# Optimizing a Trainium2 kernel written in Bass

```python
import jax, jax.numpy as jnp
from jax import lax
import numpy as np

D_MODEL = 1024
BATCH = 1
SEQ = 256
DEPTH = 2

CHUNK = 64
Q_BLOCK = 128
RMS_EPS = 1e-6

FOX_HEADS = 4
FOX_HEAD_DIM = 64
DSA_HEADS = 4
DSA_HEAD_DIM = 64
DSA_KV_RANK = 128
IDX_HEADS = 8
IDX_HEAD_DIM = 32
IDX_TOPK = 256
RWKV_HEADS = 8
RWKV_HEAD_DIM = 64
RWKV_W_LORA = 64
RWKV_A_LORA = 64
RWKV_V_LORA = 32
RWKV_G_LORA = 128
RWKV_LN_EPS = 64e-5

FOX_W = FOX_HEADS * FOX_HEAD_DIM
DSA_W = DSA_HEADS * DSA_HEAD_DIM
RWKV_W = RWKV_HEADS * RWKV_HEAD_DIM
N_BRANCH = 3
GATE_W = N_BRANCH * D_MODEL

D_FF_DENSE = 2816
N_EXPERTS = 8
TOP_K_EXPERTS = 2
D_FF_EXPERT = 3584

FOX_COLS = (FOX_W, FOX_W, FOX_W, FOX_HEADS)
DSA_COLS = (DSA_W, DSA_KV_RANK, IDX_HEADS * IDX_HEAD_DIM, IDX_HEAD_DIM, IDX_HEADS)
RWKV_COLS = (RWKV_W, RWKV_W, RWKV_W, RWKV_W_LORA, RWKV_A_LORA, RWKV_G_LORA)
FOX_IN = sum(FOX_COLS)
DSA_IN = sum(DSA_COLS)
RWKV_IN = sum(RWKV_COLS)
D_IN = FOX_IN + DSA_IN + RWKV_IN + GATE_W

kernel_name = "hybrid_fox_dsa_rwkv7_moe_trunk"

def _split(t, sizes):
    idx = [int(i) for i in np.cumsum(sizes)[:-1]]
    return jnp.split(t, idx, axis=-1)

def rmsnorm(x, g):
    xf = x.astype(jnp.float32)
    y = xf * lax.rsqrt(jnp.mean(xf * xf, axis=-1, keepdims=True) + RMS_EPS)
    return (y * g.astype(jnp.float32)).astype(x.dtype)

def token_shift_mix(p, mu):
    prev = jnp.pad(p, ((0, 0), (1, 0), (0, 0)))[:, :-1]
    return p + (prev - p) * mu

def fox_attention(q, k, v, f_logit, f_bias):
    B, S, H, Dh = q.shape
    log_f = jax.nn.log_sigmoid(f_logit.astype(jnp.float32) + f_bias.astype(jnp.float32))
    F = jnp.cumsum(log_f, axis=1).transpose(0, 2, 1)
    kpos = jnp.arange(S)
    scale = Dh ** -0.5

    def block(i):
        s0 = i * Q_BLOCK
        qb = lax.dynamic_slice_in_dim(q, s0, Q_BLOCK, axis=1)
        Fq = lax.dynamic_slice_in_dim(F, s0, Q_BLOCK, axis=2)
        logits = (jnp.einsum('bqhd,bkhd->bhqk', qb, k).astype(jnp.float32) * scale
                  + Fq[..., None] - F[:, :, None, :])
        qpos = s0 + jnp.arange(Q_BLOCK)
        logits = jnp.where(kpos[None, :] <= qpos[:, None], logits, -jnp.inf)
        p = jax.nn.softmax(logits, axis=-1).astype(v.dtype)
        return jnp.einsum('bhqk,bkhd->bqhd', p, v)

    out = lax.map(block, jnp.arange(S // Q_BLOCK))
    return out.transpose(1, 0, 2, 3, 4).reshape(B, S, H * Dh)

def dsa_attention(q, c_kv, q_idx, k_idx, w_idx, w_uk, w_uv, topk):
    B, S, H, Dh = q.shape
    q_lat = jnp.einsum('bshd,hdr->bshr', q, w_uk)
    key_chunk = jnp.arange(S) // CHUNK
    idx_scale = (IDX_HEADS * IDX_HEAD_DIM) ** -0.5
    scale = Dh ** -0.5

    def block(i):
        s0 = i * Q_BLOCK
        qi = lax.dynamic_slice_in_dim(q_idx, s0, Q_BLOCK, axis=1)
        wi = lax.dynamic_slice_in_dim(w_idx, s0, Q_BLOCK, axis=1)
        ql = lax.dynamic_slice_in_dim(q_lat, s0, Q_BLOCK, axis=1)
        rel = jax.nn.relu(jnp.einsum('bqhd,bkd->bqhk', qi, k_idx).astype(jnp.float32))
        score = jnp.einsum('bqhk,bqh->bqk', rel, wi.astype(jnp.float32)) * idx_scale
        q_chunk = (s0 + jnp.arange(Q_BLOCK)) // CHUNK
        score = jnp.where(key_chunk[None, :] <= q_chunk[:, None], score, -jnp.inf)
        top_s, top_i = lax.top_k(score, topk)
        valid = jnp.isfinite(top_s)
        c_sel = jax.vmap(lambda c, ix: c[ix])(c_kv, top_i)
        logits = jnp.einsum('bqhr,bqkr->bqhk', ql, c_sel).astype(jnp.float32) * scale
        logits = jnp.where(valid[:, :, None, :], logits, -jnp.inf)
        p = jax.nn.softmax(logits, axis=-1).astype(c_sel.dtype)
        o_lat = jnp.einsum('bqhk,bqkr->bqhr', p, c_sel)
        return jnp.einsum('bqhr,hrd->bqhd', o_lat, w_uv)

    out = lax.map(block, jnp.arange(S // Q_BLOCK))
    return out.transpose(1, 0, 2, 3, 4).reshape(B, S, H * Dh)

def rwkv7_scan(r, w, k, v, kk, a):
    B, S, H, N = r.shape

    def step(state, inp):
        r_t, w_t, k_t, v_t, kk_t, a_t = inp
        sa = jnp.einsum('bhvk,bhk->bhv', state, -kk_t)
        state = (state * w_t[:, :, None, :] + sa[..., None] * (kk_t * a_t)[:, :, None, :]
                 + v_t[..., None] * k_t[:, :, None, :])
        return state, jnp.einsum('bhvk,bhk->bhv', state, r_t)

    xs = tuple(jnp.moveaxis(t, 1, 0) for t in (r, w, k, v, kk, a))
    _, y = lax.scan(step, jnp.zeros((B, H, N, N), jnp.float32), xs)
    return jnp.moveaxis(y, 0, 1)

def rwkv7_time_mix(p, mu, w0, w_up, a0, a_up, g_up, k_k, k_a, r_k, ln_g, ln_b, v_first, v_res_logit):
    B, S, _ = p.shape
    f32 = jnp.float32
    r, k, v, wl, al, gl = [t.astype(f32) for t in _split(token_shift_mix(p, mu), RWKV_COLS)]
    if v_first is None:
        v_first = v
    else:
        v = v + (v_first - v) * jax.nn.sigmoid(v_res_logit.astype(f32))
    log_w = -jax.nn.softplus(-(w0 + jnp.tanh(wl) @ w_up)) - 0.5
    decay = jnp.exp(-jnp.exp(log_w))
    a = jax.nn.sigmoid(a0 + al @ a_up)
    g = jax.nn.sigmoid(gl) @ g_up
    heads = lambda t: t.reshape(B, S, RWKV_HEADS, RWKV_HEAD_DIM)
    kk = heads(k * k_k)
    kk = kk / jnp.sqrt(jnp.sum(kk * kk, axis=-1, keepdims=True) + 1e-12)
    k = k * (1.0 + (a - 1.0) * k_a)
    rh, kh, vh = heads(r), heads(k), heads(v)
    y = rwkv7_scan(rh, heads(decay), kh, vh, kk, heads(a))
    mean = jnp.mean(y, axis=-1, keepdims=True)
    var = jnp.mean(jnp.square(y - mean), axis=-1, keepdims=True)
    y = ((y - mean) * lax.rsqrt(var + RWKV_LN_EPS)).reshape(B, S, RWKV_W) * ln_g + ln_b
    bonus = (jnp.sum(rh * kh * r_k, axis=-1, keepdims=True) * vh).reshape(B, S, RWKV_W)
    return ((y + bonus) * g).astype(p.dtype), v_first

def swiglu(h, w_gate, w_up, w_down):
    return (jax.nn.silu(h @ w_gate) * (h @ w_up)) @ w_down

def moe_ffn(h, router_w, router_b, w_gate, w_up, w_down):
    logits = (h @ router_w).astype(jnp.float32) + router_b.astype(jnp.float32)
    top_v, top_i = lax.top_k(logits, TOP_K_EXPERTS)
    top_p = jax.nn.softmax(top_v, axis=-1)
    gates = jnp.sum(jax.nn.one_hot(top_i, N_EXPERTS, dtype=jnp.float32) * top_p[..., None], axis=-2)
    gates = gates.astype(h.dtype)
    y = jnp.zeros_like(h)
    for e in range(N_EXPERTS):
        y = y + gates[..., e:e + 1] * swiglu(h, w_gate[e], w_up[e], w_down[e])
    return y

def setup_inputs(seed: int = 0) -> dict:
    key = jax.random.key(seed)
    ks = iter(list(jax.random.split(key, 48)))
    f = jnp.float32
    n_dense = (DEPTH + 1) // 2
    n_moe = DEPTH // 2

    def nrm(shape, fan_in, s=1.0):
        return jax.random.normal(next(ks), shape, f) * (s * fan_in ** -0.5)

    def gain(shape):
        return 1.0 + 0.01 * jax.random.normal(next(ks), shape, f)

    def small(shape, s=0.01, c=0.0):
        return c + s * jax.random.normal(next(ks), shape, f)

    def unif(shape, lo, hi):
        return jax.random.uniform(next(ks), shape, f, lo, hi)

    return {
        "x": jax.random.normal(next(ks), (BATCH, SEQ, D_MODEL), f),
        "w_in": nrm((DEPTH, D_MODEL, D_IN), D_MODEL),
        "b_gate": small((DEPTH, GATE_W)),
        "g_mix": gain((DEPTH, D_MODEL)),
        "fox_f_bias": unif((DEPTH, FOX_HEADS), 1.0, 4.0),
        "dsa_kv_norm": gain((DEPTH, DSA_KV_RANK)),
        "dsa_w_uk": nrm((DEPTH, DSA_HEADS, DSA_HEAD_DIM, DSA_KV_RANK), DSA_KV_RANK),
        "dsa_w_uv": nrm((DEPTH, DSA_HEADS, DSA_KV_RANK, DSA_HEAD_DIM), DSA_KV_RANK),
        "rwkv_mu": unif((DEPTH, RWKV_IN), 0.0, 1.0),
        "rwkv_w0": unif((DEPTH, RWKV_W), -6.0, -1.0),
        "rwkv_w_up": nrm((DEPTH, RWKV_W_LORA, RWKV_W), RWKV_W_LORA, 0.5),
        "rwkv_a0": small((DEPTH, RWKV_W), 0.1),
        "rwkv_a_up": nrm((DEPTH, RWKV_A_LORA, RWKV_W), RWKV_A_LORA),
        "rwkv_g_up": nrm((DEPTH, RWKV_G_LORA, RWKV_W), RWKV_G_LORA),
        "rwkv_k_k": small((DEPTH, RWKV_W), 0.02, 0.85),
        "rwkv_k_a": small((DEPTH, RWKV_W), 0.02, 1.0),
        "rwkv_r_k": small((DEPTH, RWKV_HEADS, RWKV_HEAD_DIM), 0.1),
        "rwkv_ln_g": gain((DEPTH, RWKV_W)),
        "rwkv_ln_b": small((DEPTH, RWKV_W)),
        "vres_down": nrm((DEPTH - 1, D_MODEL, RWKV_V_LORA), D_MODEL),
        "vres_mu": unif((DEPTH - 1, RWKV_V_LORA), 0.0, 1.0),
        "vres_up": nrm((DEPTH - 1, RWKV_V_LORA, RWKV_W), RWKV_V_LORA),
        "vres_v0": small((DEPTH - 1, RWKV_W), 0.1, 0.5),
        "p_fox": nrm((DEPTH, FOX_W, D_MODEL), FOX_W),
        "p_dsa": nrm((DEPTH, DSA_W, D_MODEL), DSA_W),
        "p_rwkv": nrm((DEPTH, RWKV_W, D_MODEL), RWKV_W),
        "w_out": nrm((DEPTH, D_MODEL, D_MODEL), D_MODEL),
        "g_ffn": gain((DEPTH, D_MODEL)),
        "ffn_w_gate": nrm((n_dense, D_MODEL, D_FF_DENSE), D_MODEL),
        "ffn_w_up": nrm((n_dense, D_MODEL, D_FF_DENSE), D_MODEL),
        "ffn_w_down": nrm((n_dense, D_FF_DENSE, D_MODEL), D_FF_DENSE),
        "router_w": nrm((n_moe, D_MODEL, N_EXPERTS), D_MODEL),
        "router_b": small((n_moe, N_EXPERTS)),
        "moe_w_gate": nrm((n_moe, N_EXPERTS, D_MODEL, D_FF_EXPERT), D_MODEL),
        "moe_w_up": nrm((n_moe, N_EXPERTS, D_MODEL, D_FF_EXPERT), D_MODEL),
        "moe_w_down": nrm((n_moe, N_EXPERTS, D_FF_EXPERT, D_MODEL), D_FF_EXPERT),
        "g_final": gain((D_MODEL,)),
    }

def reference(x, w_in, b_gate, g_mix, fox_f_bias, dsa_kv_norm, dsa_w_uk, dsa_w_uv,
              rwkv_mu, rwkv_w0, rwkv_w_up, rwkv_a0, rwkv_a_up, rwkv_g_up, rwkv_k_k, rwkv_k_a,
              rwkv_r_k, rwkv_ln_g, rwkv_ln_b, vres_down, vres_mu, vres_up, vres_v0,
              p_fox, p_dsa, p_rwkv, w_out, g_ffn, ffn_w_gate, ffn_w_up, ffn_w_down,
              router_w, router_b, moe_w_gate, moe_w_up, moe_w_down, g_final):
    B, S, _ = x.shape
    topk = min(IDX_TOPK, S // 4)
    v_first = None
    for l in range(DEPTH):
        h = rmsnorm(x, g_mix[l])
        fox_p, dsa_p, rwkv_p, gate_p = _split(h @ w_in[l], (FOX_IN, DSA_IN, RWKV_IN, GATE_W))

        fq, fk, fv, f_logit = _split(fox_p, FOX_COLS)
        fh = lambda t: t.reshape(B, S, FOX_HEADS, FOX_HEAD_DIM)
        o_fox = fox_attention(fh(fq), fh(fk), fh(fv), f_logit, fox_f_bias[l])

        dq, dckv, diq, dik, diw = _split(dsa_p, DSA_COLS)
        o_dsa = dsa_attention(dq.reshape(B, S, DSA_HEADS, DSA_HEAD_DIM),
                              rmsnorm(dckv, dsa_kv_norm[l]),
                              diq.reshape(B, S, IDX_HEADS, IDX_HEAD_DIM), dik, diw,
                              dsa_w_uk[l], dsa_w_uv[l], topk)

        if l == 0:
            v_res_logit = None
        else:
            vl = token_shift_mix(h @ vres_down[l - 1], vres_mu[l - 1])
            v_res_logit = vres_v0[l - 1] + vl @ vres_up[l - 1]
        o_rwkv, v_first = rwkv7_time_mix(rwkv_p, rwkv_mu[l], rwkv_w0[l], rwkv_w_up[l], rwkv_a0[l],
                                         rwkv_a_up[l], rwkv_g_up[l], rwkv_k_k[l], rwkv_k_a[l],
                                         rwkv_r_k[l], rwkv_ln_g[l], rwkv_ln_b[l], v_first, v_res_logit)

        gates = jax.nn.sigmoid((gate_p + b_gate[l]).astype(jnp.float32)).astype(x.dtype)
        gates = gates.reshape(B, S, N_BRANCH, D_MODEL)
        merged = (gates[:, :, 0] * (o_fox @ p_fox[l])
                  + gates[:, :, 1] * (o_dsa @ p_dsa[l])
                  + gates[:, :, 2] * (o_rwkv @ p_rwkv[l]))
        x = x + merged @ w_out[l]

        h2 = rmsnorm(x, g_ffn[l])
        if l % 2 == 0:
            y = swiglu(h2, ffn_w_gate[l // 2], ffn_w_up[l // 2], ffn_w_down[l // 2])
        else:
            y = moe_ffn(h2, router_w[l // 2], router_b[l // 2],
                        moe_w_gate[l // 2], moe_w_up[l // 2], moe_w_down[l // 2])
        x = x + y
    return rmsnorm(x, g_final)


_drawn_inputs = setup_inputs


def setup_inputs(seed=0):
    import zlib

    import numpy as np

    out = dict(_drawn_inputs(seed))
    spreads = {}
    factors = {'b_gate': 7.67,
     'dsa_kv_norm': 7.134,
     'rwkv_k_a': 3.081,
     'rwkv_ln_g': 4.349,
     'rwkv_ln_b': 2.674,
     'g_ffn': 2.704,
     'g_final': 28.857,
     'vres_v0': 3.099,
     'router_b': 8.0}
    for name, (base, spread) in spreads.items():
        noise = np.random.default_rng([zlib.crc32(name.encode()), seed]).standard_normal(out[name].shape)
        drawn = base * np.exp(spread * noise) if base else spread * noise
        out[name] = __import__('jax').numpy.asarray(drawn.astype(out[name].dtype))
    for name, factor in factors.items():
        out[name] = (out[name] * factor).astype(out[name].dtype)
    return out
```

```python
from contextlib import ExitStack

import concourse.bass as bass
from concourse import mybir

F32 = mybir.dt.float32
I32 = mybir.dt.int32
ALU = mybir.AluOpType
ACT = mybir.ActivationFunctionType
AX = mybir.AxisListType.X

P = 128
D = 1024
KD = D // P
T = 256
NT = T // P
DEPTH = 2
CHUNK = 64
EPS = 1e-6
FH, DH, RH, IH = 4, 4, 8, 8
HD = 64
TOPK = min(256, T // 4)
W_FOX = FH * HD
W_DSA = DH * HD
W_RW = RH * HD
KV = 128
FOX0 = 0
DSA0 = 3 * W_FOX + FH
RW0 = DSA0 + W_DSA + KV + IH * 32 + 32 + IH
GATE0 = RW0 + 3 * W_RW + 64 + 64 + 128
FF = 2816
NE = 8
FFE = 3584
NITEM = 16
LN_EPS = 64e-5
DECAY = 0.6065306597126334
NEG = -1e30
SLOT = KD * 512


def trunk(nc, a, out):
    ctx = ExitStack()
    with ctx:
        base = (nc.sbuf_base + 63) // 64 * 64
        end = nc.sbuf_usable_end
        cursor = [base]

        def place(name, shape, at=None, dt=F32):
            n = 4
            for s in shape[1:]:
                n *= s
            if at is None:
                at = cursor[0]
                cursor[0] = (at + n + 31) // 32 * 32
            assert at + n <= end, (name, at + n, end)
            return nc.alloc_sbuf_tensor_at(name, shape, dt, offset=at)

        def overlay(at, limit, items):
            made = {}
            for name, shape in items:
                n = 4
                for s in shape[1:]:
                    n *= s
                made[name] = place(name, shape, at)
                at += (n + 31) // 32 * 32
                assert at <= limit, (name, at, limit)
            return made

        ident = place("ident", [P, P])
        ones = place("ones", [P, P])
        blk = place("blk", [P, P])
        upper = place("upper", [P, 4, P])
        level = place("level", [P, 7, P])
        fmask = place("fmask", [P, NT, T])
        dmask = place("dmask", [P, NT, T])
        iota = place("iota", [P, P])
        tab = place("tab", [1, 2 * NITEM], dt=I32)
        pidx = place("pidx", [P, 1])
        cst = place("cst", [P, 8])
        rs = place("rs", [P, T])
        VA = place("VA", [P, P])
        VB = place("VB", [P, 64])
        fbias = place("fbias", [4, DEPTH])
        vlmu = place("vlmu", [32, 1])
        vl = place("vl", [32, T])
        w_lora = place("w_lora", [P, DEPTH, W_RW])
        g_lora = place("g_lora", [P, DEPTH, W_RW])
        v_lora = place("v_lora", [32, W_RW])
        v_down = place("v_down", [P, KD, 32])
        w_uk = place("w_uk", [P, DEPTH, 2, KV])
        w_uv = place("w_uv", [P, DEPTH, DH, HD])
        w_rt = place("w_rt", [P, KD, NE])
        b_rt = place("b_rt", [1, NE])
        x = place("x", [P, KD, T])
        h = place("h", [P, KD, T])
        sq = place("sq", [P, KD, T])
        ring0 = cursor[0]
        NS, NSE = 3, 7
        slots = [place(f"slot{i}", [P, SLOT], ring0 + i * SLOT * 4) for i in range(NSE)]
        moe0 = ring0 + NSE * SLOT * 4
        r1 = ring0 + NS * SLOT * 4
        L1 = [("raw", [P, 15, T + 1]), ("sg", [P, 4, T]), ("cum", [P, 4, 2, P + 1]),
              ("ep", [P, 4, 2, P + 1]), ("em", [P, 4, 2, P])]
        n1 = 32768
        R1 = overlay(r1, r1 + n1, L1)
        raw, sg, cum, ep, em = (R1[n] for n in ("raw", "sg", "cum", "ep", "em"))
        Bm = place("Bm", [P, 16, 4, P], r1)
        gates = place("gates", [P, 24, T], r1)
        hid = place("hid", [P, 4, T], r1)
        hsig = place("hsig", [P, 4, T], r1 + 8192)
        r2 = r1 + n1
        n2 = 32768
        R2 = overlay(r2, r2 + n2, [("mx", [P, 14, T]), ("aa", [P, 4, T]), ("kk", [P, 4, T]),
                                   ("kp", [P, 4, T]), ("bb", [P, 4, T])])
        mx, aa, kk, kp, bb = (R2[n] for n in ("mx", "aa", "kk", "kp", "bb"))
        S2 = overlay(r2, r2 + n2, [("Ti", [P, 16, P]), ("Tt", [P, 16, P]), ("Xs", [P, 16, P]),
                                   ("Lo", [P, 16, P])])
        Ti, Tt, Xs, Lo = (S2[n] for n in ("Ti", "Tt", "Xs", "Lo"))
        r3 = r2 + n2
        n3 = 34880
        R3 = overlay(r3, r3 + n3, [("AR", [P, 4, 2, 2, P]), ("BK", [P, 4, 2, 2, P]),
                                   ("vt", [P, 2, W_RW]), ("bt", [P, W_RW]), ("kt", [P, W_RW]),
                                   ("Gs", [P, W_RW]), ("SA", [P, W_RW]), ("Zs", [P, 4, HD]),
                                   ("yT", [P, 4, T]), ("fac", [P, 4, 4]), ("zf", [P, 4])])
        AR, BK, vt, bt, kt, Gs, SA, Zs, yT, fac, zf = (R3[n] for n in (
            "AR", "BK", "vt", "bt", "kt", "Gs", "SA", "Zs", "yT", "fac", "zf"))
        kstd = place("kstd", [P, 4, T], r1 + 15424 + 4096 + 2 * 4128)
        A3 = overlay(r3, r3 + n3, [("L0", [P, 4, P]), ("L1", [P, 4, T]), ("PT0", [P, 4, T]),
                                   ("PT1", [P, 4, P]), ("fq", [P, 2, T]), ("fk", [P, 2, T]),
                                   ("fv", [P, NT, W_FOX]), ("ql", [P, 4, T]), ("ol", [P, 4, T]),
                                   ("rel", [P, 2, 512]), ("dq", [P, 2, T])])
        L0, L1b, PT0, PT1, fq, fk, fv, ql, ol, rel, dq = (A3[n] for n in (
            "L0", "L1", "PT0", "PT1", "fq", "fk", "fv", "ql", "ol", "rel", "dq"))
        A1 = overlay(r1 + 15424, r1 + n1, [("fz", [4, T]), ("ft", [4, T]), ("F8", [4, T]),
                                           ("nF8", [4, T]), ("cc", [P, T]), ("ccs", [P, T]),
                                           ("cn", [P, T]), ("ct", [P, NT, P]), ("iq", [P, 2, T]),
                                           ("ik", [P, T]), ("iw", [P, NT, IH]), ("rels", [P, 2, T])])
        fz, ft, F8, nF8, cc, ccs, cn, ct, iq, ik, iw, rels = (A1[n] for n in (
            "fz", "ft", "F8", "nF8", "cc", "ccs", "cn", "ct", "iq", "ik", "iw", "rels"))
        A2 = overlay(r2 + 14336, r2 + n2, [("sc", [P, NT, T]), ("wk", [P, NT, T]), ("eq", [P, NT, T]),
                                           ("cs", [P, NT, T]), ("m8", [P, NT, 8]), ("cnt", [P, NT]),
                                           ("st", [P, 4, 4, 4]),
                                           ("crin", [P, T]), ("wrep", [P, KD, P])])
        sc, wk, eq, cs, m8, cnt, st, crin, wrep = (A2[n] for n in (
            "sc", "wk", "eq", "cs", "m8", "cnt", "st", "crin", "wrep"))
        r4 = r3 + n3
        R4 = overlay(r4, end, [("vf", [P, 4, T]), ("oF", [P, 2, T]), ("oD", [P, 2, T])])
        vf, oF, oD = (R4[n] for n in ("vf", "oF", "oD"))
        ysq = place("ysq", [P, 4, T], r3 + 8192)
        ym = place("ym", [P, 4, T], r3 + 8192 + 4096)
        mtmp = place("mtmp", [P, 4, 2, T], r2)
        bon = sq[:, 0:4, :]
        gg = sq[:, 4:8, :]
        xt = place("xt", [P, NT, D], r1)
        rows = place("rows", [P, 2, P], r2)
        iota_i = place("iota_i", [P, P], r2 + 1024, dt=I32)
        pidx_i = place("pidx_i", [P, 1], r2 + 1536, dt=I32)
        E = overlay(moe0, end, [("ht", [P, NT, D]), ("xg", [P, KD, P]), ("aT", [P, 2, 4, P]),
                                ("gs", [P, 2, 512]), ("av", [P, 2, 512]), ("Ys", [P, D]),
                                ("Sl", [P, NT, P]), ("Sp", [P, NT, P]), ("SpT", [P, T]),
                                ("lg", [P, NT, NE]), ("mr", [P, NT, NE]), ("sl", [P, NT, NE]),
                                ("eqr", [P, NT, NE]), ("csr", [P, NT, NE]), ("nr", [P, 4]),
                                ("gt", [P, NT, NE]), ("ex", [P, NT, NE]), ("pos", [P, NT, NE]),
                                ("nb", [P, 2, NE]), ("cb", [P, NE]), ("ecol", [P, 2]),
                                ("cmp", [P, NE]), ("ebc", [P, 2, NITEM]), ("oh", [P, NITEM, NE]),
                                ("pr", [P, NITEM, NE]), ("posI", [P, NT, NITEM]),
                                ("gateI", [P, NT, NITEM])])
        (ht, xg, aT, gs, av, Ys, Sl, Sp, SpT, lg, mr, sl, eqr, csr, nr, gt, ex, pos, nb, cb, ecol,
         cmp, ebc, oh, pr, posI, gateI) = (E[n] for n in (
             "ht", "xg", "aT", "gs", "av", "Ys", "Sl", "Sp", "SpT", "lg", "mr", "sl", "eqr", "csr",
             "nr", "gt", "ex", "pos", "nb", "cb", "ecol", "cmp", "ebc", "oh", "pr", "posI",
             "gateI"))
        banks = [ctx.enter_context(nc.psum_tensor(f"bank{i}", [P, 512], F32)) for i in range(8)]

        def sem(name):
            return ctx.enter_context(nc.semaphore(name))

        S = {n: sem(n) for n in (
            "consts", "rows_in", "x_in", "smallw_in", "vecs", "sq_ready", "std_ready", "h_ready",
            "x_ready", "fox_z", "fox_e", "fox_l", "fox_F", "max_ready", "exp_ready", "p_ready",
            "css", "cstd", "cn_ready", "sel_ready", "shift_ready", "tanh_ready", "sgm_ready",
            "cum_ready", "kks", "kstd", "kk_ready", "rk_ready", "exps_ready", "ar_ready",
            "v_ready", "lo_ready", "x_copied", "gn_ready", "gsq", "gstd", "o_ready", "merged",
            "rel_used", "hid_sig", "hid_ready", "gates_in", "hT_done", "route", "route_e", "route_x",
            "route_g", "route_n", "route_c", "route_t", "sel_item", "xT_item", "gs_item", "av_item",
            "out_tok", "stored", "vector_step", "scalar_step", "pool_step", "moe_up", "moe_done",
            "tab_ready", "y_item", "yscat", "down_done", "fin_ready", "x_final", "pa_half", "ik_w")}
        slot_full = [sem(f"slot_full{i}") for i in range(NSE)]
        bank_full = [sem(f"bank_full{i}") for i in range(8)]
        bank_done = [sem(f"bank_done{i}") for i in range(8)]

        def need(eng, name, value):
            assert value > 0
            eng.wait_ge(S[name], value)

        def stepper(eng, name):
            n = [0]

            def step(ins):
                ins.then_inc(S[name], 1)
                n[0] += 1

            def sync():
                if n[0]:
                    eng.wait_ge(S[name], n[0])
            return step, sync

        turn = [0]
        fills = [0] * 8
        filling = {}

        def open_bank(pe, name):
            b = turn[0] % 8
            turn[0] += 1
            if fills[b]:
                pe.wait_ge(bank_done[b], fills[b])
            fills[b] += 1
            filling[name] = (b, fills[b])
            return banks[b]

        def close_bank(ins, name):
            ins.then_inc(bank_full[filling[name][0]], 1)

        def take(eng, name):
            b, n = filling[name]
            eng.wait_ge(bank_full[b], n)
            return banks[b]

        def done(ins, name):
            ins.then_inc(bank_done[filling[name][0]], 1)

        def need_sb(eng, name):
            b, n = filling[name]
            eng.wait_ge(bank_done[b], n)

        sturn = [0]
        loads = [0] * NSE
        load_at = {}

        def open_slot(pe, name):
            s = sturn[0] % NS
            sturn[0] += 1
            loads[s] += 1
            load_at[name] = (s, loads[s])
            pe.wait_ge(slot_full[s], 16 * loads[s])
            return slots[s]

        released = {}

        def free_slot(name, bank_name):
            b, n = filling[bank_name]
            released[name] = (bank_full[b], n)

        w_in = a["w_in"]

        def c3(t, k, n):
            return t[:, 0:k * n].rearrange("p (k n) -> p k n", k=k)

        def v2(bank):
            return bank[:, :].rearrange("p (m t) -> p m t", m=2)

        def v4(bank):
            return bank[:, :].rearrange("p (m t) -> p m t", m=4)

        block = ctx.enter_context(nc.Block())
        EPER = [5, 4, 5, 4, 6, 4, 1, 1]
        NJ = FFE // 512
        DOWN0 = FF // 512 + 1
        GI = 2
        DI = FF // 512
        loop_fill = {}

        @block.tensor
        def _(pe):
            mm = nc.tensor.matmul

            need(pe, "consts", 1)
            need(pe, "rows_in", 16 * 15)
            b = open_bank(pe, "vecs")
            nc.tensor.transpose(b[:, 0:126], rows[0:126, 0, :], ident[0:126, 0:126])
            close_bank(nc.tensor.transpose(b[:, 128:180], rows[0:52, 1, :], ident[0:52, 0:52]), "vecs")
            need(pe, "x_in", 16)
            for tt in range(NT):
                for g in range(2):
                    n = f"x{tt}{g}"
                    b = v4(open_bank(pe, n))
                    for j in range(4):
                        k = 4 * g + j
                        ins = nc.tensor.transpose(b[:, j, :], xt[:, tt, k * P:(k + 1) * P], ident[:, :])
                    close_bank(ins, n)
            need(pe, "smallw_in", 16 * 12)

            def norm(n):
                b = open_bank(pe, f"ss{n}")
                need(pe, "sq_ready", n + 1)
                for k in range(KD):
                    ins = mm(b[:, 0:T], ones[:, :], sq[:, k, :], start=k == 0, stop=k == KD - 1)
                close_bank(ins, f"ss{n}")
                need(pe, "h_ready", KD * (n + 1))

            def unit(o, w, c, n, rhs=h, nk=KD):
                for k in range(nk):
                    ins = mm(o, w[:, k, c:c + n], rhs[:, k, :], start=k == 0, stop=k == nk - 1)
                return ins

            def pair(name, w, c, wide=P):
                b = v2(open_bank(pe, name))
                unit(b[:, 0, :], w, c, P)
                ins = unit(b[:, 1, :], w, c + P, P)
                close_bank(ins, name)
                return ins

            def tokens(o, w, c, n):
                for tt in range(NT):
                    for k in range(KD):
                        ins = mm(o[:, tt, 0:n], h[:, k, tt * P:(tt + 1) * P], w[:, k, c:c + n],
                                 start=k == 0, stop=k == KD - 1)
                return ins

            def probs_t(nm):
                need(pe, "p_ready", 2 * (2 * l + (nm == "d")) + 1)
                n = f"{l}{nm}t0"
                b = v4(open_bank(pe, n))
                for hh in range(4):
                    ins = nc.tensor.transpose(b[:, hh, :], L0[:, hh, :], ident[:, :])
                close_bank(ins, n)
                need(pe, "p_ready", 2 * (2 * l + (nm == "d")) + 2)
                for kb in range(2):
                    n = f"{l}{nm}t{1 + kb}"
                    b = v4(open_bank(pe, n))
                    for hh in range(4):
                        ins = nc.tensor.transpose(b[:, hh, :], L1b[:, hh, kb * P:(kb + 1) * P], ident[:, :])
                    close_bank(ins, n)

            for l in range(DEPTH):
                L = f"{l}"
                norm(2 * l)
                w = c3(open_slot(pe, L + "w0"), KD, 512)
                pair(L + "fq", w, 0)
                pair(L + "fk", w, 256)
                free_slot(L + "w0", L + "fk")
                w = c3(open_slot(pe, L + "w1"), KD, 260)
                b = v2(open_bank(pe, L + "fv"))
                close_bank(tokens(b, w, 0, 256), L + "fv")
                b = open_bank(pe, L + "ff")
                ins = unit(b[0:4, 0:T], w, 256, 4)
                close_bank(ins, L + "ff")
                b = v2(open_bank(pe, L + "cc"))
                wn = c3(open_slot(pe, L + "w2"), KD, 384)
                ins = unit(b[:, 0, :], wn, 256, P)
                close_bank(ins, L + "cc")
                pair(L + "dq", wn, 0)
                free_slot(L + "w1", L + "ff")
                free_slot(L + "w2", L + "dq")
                w = c3(open_slot(pe, L + "w3"), KD, 296)
                pair(L + "iq", w, 0)
                b = v2(open_bank(pe, L + "ik"))
                need(pe, "ik_w", l + 1)
                for k in range(KD):
                    ins = mm(b[:, 0, :], wrep[:, k, :], h[:, k, :], start=k == 0, stop=k == KD - 1)
                close_bank(ins, L + "ik")
                b = open_bank(pe, L + "iw")
                bw = b[:, 0:2 * IH].rearrange("p (t e) -> p t e", t=2)
                close_bank(tokens(bw, w, 288, IH), L + "iw")
                free_slot(L + "w3", L + "iw")

                need_sb(pe, L + "iq")
                need_sb(pe, L + "ik")
                for qt in range(NT):
                    nk = P * (qt + 1)
                    for r in range(4):
                        n = f"{l}rel{qt}{r}"
                        b = open_bank(pe, n)
                        o = 32 * r
                        for j in range(2):
                            ins = mm(b[:, j * nk:(j + 1) * nk], iq[o:o + 32, j, qt * P:(qt + 1) * P],
                                     ik[o:o + 32, 0:nk], start=True, stop=True)
                        close_bank(ins, n)
                b = open_bank(pe, L + "css")
                need(pe, "css", l + 1)
                close_bank(mm(b[:, 0:T], ones[:, :], ccs[:, :], start=True, stop=True), L + "css")
                need_sb(pe, L + "dq")
                for j in range(2):
                    b = v2(open_bank(pe, f"{l}ql{j}"))
                    for g in range(2):
                        ins = mm(b[:, g, :], w_uk[64 * j:64 * j + 64, l, g, :], dq[64 * j:64 * j + 64, g, :],
                                 start=True, stop=True)
                    close_bank(ins, f"{l}ql{j}")

                w = c3(open_slot(pe, L + "w4"), KD, 512)
                pair(L + "r0", w, 0)
                pair(L + "r1", w, 256)
                free_slot(L + "w4", L + "r1")

                need_sb(pe, L + "fq")
                need_sb(pe, L + "fk")
                need(pe, "fox_F", l + 1)

                def fox_scores(o, hh, qt, nk):
                    p0 = 64 * (hh % 2)
                    one_h = ident[0:4, hh:hh + 1]
                    mm(o, fq[p0:p0 + 64, hh // 2, qt * P:(qt + 1) * P], fk[p0:p0 + 64, hh // 2, 0:nk],
                       start=True, stop=False)
                    mm(o, F8[:, qt * P:(qt + 1) * P], one_h.broadcast_to([4, nk]), start=False, stop=False)
                    return mm(o, one_h.broadcast_to([4, P]), nF8[:, 0:nk], start=False, stop=True)

                for qt in range(NT):
                    for odd in range(2):
                        n = f"{l}fl{2 * qt + odd}"
                        b = v2(open_bank(pe, n))
                        for j in range(2):
                            ins = fox_scores(b[:, j, 0:P * (qt + 1)], 2 * j + odd, qt, P * (qt + 1))
                        close_bank(ins, n)

                w = c3(open_slot(pe, L + "w5"), KD, 512)
                pair(L + "k0", w, 0)
                pair(L + "k1", w, 256)
                free_slot(L + "w5", L + "k1")
                probs_t("f")
                w = c3(open_slot(pe, L + "w6"), KD, 512)
                pair(L + "v0", w, 0)
                need_sb(pe, L + "fv")
                for i in range(3):
                    need_sb(pe, f"{l}ft{i}")
                b = v2(open_bank(pe, L + "fo"))
                for hh in range(4):
                    p0 = 64 * (hh % 2)
                    o = b[p0:p0 + 64, hh // 2, :]
                    mm(o, fv[:, 0, hh * 64:hh * 64 + 64], PT0[:, hh, :], start=True, stop=False)
                    ins = mm(o[:, P:T], fv[:, 1, hh * 64:hh * 64 + 64], PT1[:, hh, :], start=False, stop=True)
                close_bank(ins, L + "fo")
                pair(L + "v1", w, 256)
                free_slot(L + "w6", L + "v1")
                w = c3(open_slot(pe, L + "w7"), KD, 256)
                pair(L + "wg", w, 0)
                free_slot(L + "w7", L + "wg")
                if l:
                    b = open_bank(pe, L + "vl")
                    close_bank(unit(b[0:32, 0:T], v_down, 0, 32), L + "vl")
                need(pe, "cn_ready", l + 1)
                b = open_bank(pe, L + "ct")
                for j in range(NT):
                    ins = nc.tensor.transpose(b[:, j * P:(j + 1) * P], cn[:, j * P:(j + 1) * P], ident[:, :])
                close_bank(ins, L + "ct")
                need_sb(pe, L + "ql0")
                need_sb(pe, L + "ql1")
                for qt in range(NT):
                    for odd in range(2):
                        n = f"{l}dl{2 * qt + odd}"
                        b = v2(open_bank(pe, n))
                        for j in range(2):
                            ins = mm(b[:, j, 0:P * (qt + 1)], ql[:, 2 * j + odd, qt * P:(qt + 1) * P],
                                     cn[:, 0:P * (qt + 1)], start=True, stop=True)
                        close_bank(ins, n)
                probs_t("d")
                need_sb(pe, L + "ct")
                for i in range(3):
                    need_sb(pe, f"{l}dt{i}")
                for g in range(2):
                    b = v2(open_bank(pe, f"{l}ol{g}"))
                    for j in range(2):
                        hh = 2 * g + j
                        mm(b[:, j, :], ct[:, 0, :], PT0[:, hh, :], start=True, stop=False)
                        ins = mm(b[:, j, P:T], ct[:, 1, :], PT1[:, hh, :], start=False, stop=True)
                    close_bank(ins, f"{l}ol{g}")
                need_sb(pe, L + "ol0")
                need_sb(pe, L + "ol1")
                b = v2(open_bank(pe, L + "do"))
                for hh in range(4):
                    p0 = 64 * (hh % 2)
                    ins = mm(b[p0:p0 + 64, hh // 2, :], w_uv[:, l, hh, :], ol[:, hh, :], start=True, stop=True)
                close_bank(ins, L + "do")

                need(pe, "tanh_ready", 2 * l + 1)
                for g in range(2):
                    b = v2(open_bank(pe, f"{l}zw{g}"))
                    for j in range(2):
                        c = (2 * g + j) * P
                        ins = mm(b[:, j, :], w_lora[0:64, l, c:c + P], mx[0:64, 12, :], start=True, stop=True)
                    close_bank(ins, f"{l}zw{g}")
                for g in range(2):
                    b = v2(open_bank(pe, f"{l}za{g}"))
                    for j in range(2):
                        c = (2 * g + j) * P
                        ins = mm(b[:, j, :], w_lora[64:128, l, c:c + P], mx[64:128, 12, :], start=True, stop=True)
                    close_bank(ins, f"{l}za{g}")
                need(pe, "tanh_ready", 2 * l + 2)
                for g in range(2):
                    b = v2(open_bank(pe, f"{l}zg{g}"))
                    for j in range(2):
                        c = (2 * g + j) * P
                        ins = mm(b[:, j, :], g_lora[:, l, c:c + P], mx[:, 13, :], start=True, stop=True)
                    close_bank(ins, f"{l}zg{g}")
                if l:
                    need(pe, "shift_ready", 2 * l + 2)
                    for g in range(2):
                        b = v2(open_bank(pe, f"{l}zv{g}"))
                        for j in range(2):
                            c = (2 * g + j) * P
                            ins = mm(b[:, j, :], v_lora[:, c:c + P], vl[:, :], start=True, stop=True)
                        close_bank(ins, f"{l}zv{g}")
                need(pe, "kks", l + 1)
                for g in range(2):
                    b = v2(open_bank(pe, f"{l}ks{g}"))
                    close_bank(mm(b[:, :, :], blk[:, :], bb[:, 2 * g:2 * g + 2, :], start=True, stop=True),
                               f"{l}ks{g}")
                need(pe, "v_ready", l + 1)
                for c in range(2):
                    b = v4(open_bank(pe, f"{l}vt{c}"))
                    for j in range(4):
                        ins = nc.tensor.transpose(b[:, j, :], mx[:, 8 + j, c * P:(c + 1) * P], ident[:, :])
                    close_bank(ins, f"{l}vt{c}")
                need(pe, "rk_ready", l + 1)
                for g in range(2):
                    b = v2(open_bank(pe, f"{l}bo{g}"))
                    close_bank(mm(b[:, :, :], blk[:, :], aa[:, 2 * g:2 * g + 2, :], start=True, stop=True),
                               f"{l}bo{g}")
                need(pe, "ar_ready", l + 1)
                for i, nm in enumerate(("bt", "kt")):
                    b = v4(open_bank(pe, L + nm))
                    for j in range(4):
                        ins = nc.tensor.transpose(b[:, j, :], BK[:, j, 0, i, :], ident[:, :])
                    close_bank(ins, L + nm)
                for c in range(2):
                    for hh in range(RH):
                        p0, j = 64 * (hh % 2), hh // 2
                        n = f"{l}B{c * RH + hh}"
                        b = v4(open_bank(pe, n))
                        mm(b[:, 0:2, :], BK[p0:p0 + 64, j, c, 0, :], AR[p0:p0 + 64, j, c, :, :],
                           start=True, stop=True)
                        ins = mm(b[:, 2:4, :], BK[p0:p0 + 64, j, c, 1, :], AR[p0:p0 + 64, j, c, :, :],
                                 start=True, stop=True)
                        close_bank(ins, n)
                for lev in range(7):
                    for g in range(4):
                        need(pe, "lo_ready", (l * 7 + lev) * 4 + g + 1)
                        if lev:
                            for nm in ("y", "z") if lev > 1 else ("x",):
                                need_sb(pe, f"{l}{nm}{lev - 1}{g}")
                        n = f"{l}x{lev}{g}"
                        b = v4(open_bank(pe, n))
                        for i in range(4):
                            m = 4 * g + i
                            ins = mm(b[:, i, :], Lo[:, m, :], ident[:, :] if lev == 0 else Ti[:, m, :],
                                     start=True, stop=True)
                        close_bank(ins, n)
                    if lev == 0:
                        continue
                    for g in range(4):
                        need_sb(pe, f"{l}x{lev}{g}")
                        n = f"{l}z{lev}{g}"
                        b = v4(open_bank(pe, n))
                        for i in range(4):
                            m = 4 * g + i
                            ins = mm(b[:, i, :], Xs[:, m, :], Tt[:, m, :], start=True, stop=True)
                        close_bank(ins, n)
                        if lev < 6:
                            n = f"{l}y{lev}{g}"
                            b = v4(open_bank(pe, n))
                            for i in range(4):
                                m = 4 * g + i
                                ins = mm(b[:, i, :], Tt[:, m, :], Xs[:, m, :], start=True, stop=True)
                            close_bank(ins, n)
                for g in range(4):
                    need_sb(pe, f"{l}z6{g}")
                need_sb(pe, f"{l}vt0")
                need_sb(pe, f"{l}vt1")
                need_sb(pe, L + "bt")
                need_sb(pe, L + "kt")
                for c in range(2):
                    for odd in range(2):
                        b = open_bank(pe, f"{l}G{c}{odd}")
                        p0 = 64 * odd
                        for j in range(4):
                            hh = 2 * j + odd
                            o = b[:, j * 64:j * 64 + 64]
                            ins = mm(o, Bm[:, c * RH + hh, 2, :], vt[:, c, hh * 64:hh * 64 + 64], start=True,
                                     stop=c == 0)
                            if c:
                                ins = mm(o, AR[p0:p0 + 64, j, 1, 0, :], Zs[p0:p0 + 64, j, :], start=False, stop=True)
                        close_bank(ins, f"{l}G{c}{odd}")
                    need_sb(pe, f"{l}G{c}0")
                    need_sb(pe, f"{l}G{c}1")
                    b = open_bank(pe, f"{l}SA{c}")
                    for hh in range(RH):
                        ins = mm(b[:, hh * 64:hh * 64 + 64], Tt[:, c * RH + hh, :], Gs[:, hh * 64:hh * 64 + 64],
                                 start=True, stop=True)
                    close_bank(ins, f"{l}SA{c}")
                    need_sb(pe, f"{l}SA{c}")
                    if c == 0:
                        b = open_bank(pe, L + "Z")
                        for hh in range(RH):
                            p0, j = 64 * (hh % 2), hh // 2
                            o = b[p0:p0 + 64, j * 64:j * 64 + 64]
                            mm(o, bt[:, hh * 64:hh * 64 + 64], SA[:, hh * 64:hh * 64 + 64], start=True, stop=False)
                            ins = mm(o, kt[:, hh * 64:hh * 64 + 64], vt[:, 0, hh * 64:hh * 64 + 64],
                                     start=False, stop=True)
                        close_bank(ins, L + "Z")
                    b = v4(open_bank(pe, f"{l}Y{c}"))
                    for hh in range(RH):
                        p0, j, m = 64 * (hh % 2), hh // 2, c * RH + hh
                        o = b[p0:p0 + 64, j, :]
                        mm(o, SA[:, hh * 64:hh * 64 + 64], Bm[:, m, 1, :], start=True, stop=False)
                        ins = mm(o, vt[:, c, hh * 64:hh * 64 + 64], Bm[:, m, 3, :], start=False, stop=c == 0)
                        if c:
                            ins = mm(o, Zs[p0:p0 + 64, j, :], AR[p0:p0 + 64, j, 1, 1, :], start=False, stop=True)
                    close_bank(ins, f"{l}Y{c}")
                    if c == 0:
                        need_sb(pe, L + "Z")
                need_sb(pe, f"{l}Y0")
                need_sb(pe, f"{l}Y1")
                for g in range(2):
                    b = v2(open_bank(pe, f"{l}gm{g}"))
                    close_bank(mm(b[:, :, :], blk[:, :], yT[:, 2 * g:2 * g + 2, :], start=True, stop=True),
                               f"{l}gm{g}")
                for g in range(2):
                    need(pe, "gsq", 2 * l + g + 1)
                    b = v2(open_bank(pe, f"{l}gv{g}"))
                    close_bank(mm(b[:, :, :], blk[:, :], ysq[:, 2 * g:2 * g + 2, :],
                                  start=True, stop=True), f"{l}gv{g}")

                while turn[0] % 8:
                    turn[0] += 1
                loop_fill[f"g{l}"] = (list(fills), list(loads), sturn[0])
                with pe.Fori(0, GI) as i:
                    for s in range(3):
                        si = (sturn[0] + s) % NS
                        pe.wait_ge(slot_full[si], i * 16 + 16 * (loads[si] + 1))
                        w = c3(slots[si], KD, 512)
                        for g in range(2):
                            bi = 2 * s + g
                            pe.wait_ge(bank_done[bi], i + fills[bi])
                            b = v2(banks[bi])
                            unit(b[:, 0, :], w, 256 * g, P)
                            ins = unit(b[:, 1, :], w, 256 * g + P, P)
                            ins.then_inc(bank_full[bi], 1)
                for s in range(3):
                    loads[(sturn[0] + s) % NS] += GI
                for bi in range(6):
                    fills[bi] += GI

                for nm, src, nk, ready in (("pf", oF, 2, 1), ("pd", oD, 2, 2), ("pr", yT, 4, 3)):
                    if nm == "pf":
                        w = c3(open_slot(pe, L + "pa"), 4, D)
                        need(pe, "pa_half", 16 * (l + 1))
                        need_sb(pe, L + "fo")
                        off = 0
                    elif nm == "pd":
                        need_sb(pe, L + "do")
                        off = 2
                    else:
                        w = c3(open_slot(pe, L + "pb"), 4, D)
                        need(pe, "o_ready", l + 1)
                        off = 0
                    for g in range(4):
                        n = f"{l}{nm}{g}"
                        b = v2(open_bank(pe, n))
                        for j in range(2):
                            m = 2 * g + j
                            for k in range(nk):
                                ins = mm(b[:, j, :], w[:, off + k, m * P:(m + 1) * P], src[:, k, :],
                                         start=k == 0, stop=k == nk - 1)
                        close_bank(ins, n)
                    if nm != "pf":
                        free_slot(L + ("pa" if nm == "pd" else "pb"), f"{l}{nm}3")
                need(pe, "merged", 4 * (l + 1))
                for s in range(2):
                    w = c3(open_slot(pe, f"{l}wo{s}"), KD, 512)
                    for g in range(2):
                        n = f"{l}xo{2 * s + g}"
                        b = v2(open_bank(pe, n))
                        unit(b[:, 0, :], w, 256 * g, P, rhs=sq)
                        close_bank(unit(b[:, 1, :], w, 256 * g + P, P, rhs=sq), n)
                    free_slot(f"{l}wo{s}", f"{l}xo{2 * s + 1}")

                norm(2 * l + 1)
                if l == 0:
                    while turn[0] % 8:
                        turn[0] += 1
                    loop_fill["d"] = (list(fills), list(loads), sturn[0])
                    for bi in range(4, 8):
                        pe.wait_ge(bank_done[bi], fills[bi])

                    def dense(i, nf, first, last):
                        sl3 = [(sturn[0] + s) % NS for s in range(3)]
                        for s, name in enumerate(("gate", "up")):
                            si = sl3[s]
                            pe.wait_ge(slot_full[si], 16 * (loads[si] + 1) + i * 16)
                            w = c3(slots[si], KD, nf * P)
                            for g in range(nf // 2):
                                bi = 2 * s + g
                                pe.wait_ge(bank_done[bi], fills[bi] + i)
                                b = v2(banks[bi])
                                unit(b[:, 0, :], w, 256 * g, P)
                                unit(b[:, 1, :], w, 256 * g + P, P).then_inc(bank_full[bi], 1)
                        si = sl3[2]
                        pe.wait_ge(slot_full[si], 16 * (loads[si] + 1) + i * 16)
                        w = c3(slots[si], nf, D)
                        for g in range(nf // 2):
                            pe.wait_ge(bank_done[2 + g], fills[2 + g] + i + 1)
                        for m in range(KD):
                            for k in range(nf):
                                ins = mm(v2(banks[4 + m // 2])[:, m % 2, :], w[:, k, m * P:(m + 1) * P],
                                         hid[:, k, :], start=first and k == 0, stop=last and k == nf - 1,
                                         skip_group_check=True)
                        ins.then_inc(S["down_done"], 1)

                    for bi in range(4, 8):
                        mm(banks[bi][:, :], cst[:, 0:1].broadcast_to([P, P]), cst[:, 0:1].broadcast_to([P, 512]),
                           start=True, stop=False, skip_group_check=True).then_inc(bank_full[bi], 1)
                    with pe.Fori(0, DI) as i:
                        dense(i, 4, False, False)
                    dense(DI, 2, False, True)
                    for s in range(3):
                        loads[s] += DI + 1
                    for bi in range(4):
                        fills[bi] += DI + (bi % 2 == 0)
                    for bi in range(4, 8):
                        fills[bi] += 1

            l = 1
            b = open_bank(pe, "rt")
            br = b[:, 0:2 * NE].rearrange("p (t e) -> p t e", t=2)
            for tt in range(NT):
                for k in range(KD):
                    mm(br[:, tt, :], h[:, k, tt * P:(tt + 1) * P], w_rt[:, k, :], start=k == 0, stop=False)
                ins = mm(br[:, tt, :], ones[0:1, :], b_rt[:, :], start=False, stop=True)
            close_bank(ins, "rt")
            for tt in range(NT):
                for g in range(2):
                    n = f"ht{tt}{g}"
                    b = v4(open_bank(pe, n))
                    for j in range(4):
                        k = 4 * g + j
                        ins = nc.tensor.transpose(b[:, j, :], h[:, k, tt * P:(tt + 1) * P], ident[:, :])
                    close_bank(ins, n)
            need(pe, "route_c", 1)
            b = open_bank(pe, "cn")
            mm(b[:, 0:NE], upper[:, 1, :], sl[:, 0, :], start=True, stop=True)
            mm(b[:, NE:2 * NE], upper[:, 1, :], sl[:, 1, :], start=True, stop=False)
            mm(b[:, NE:2 * NE], ones[:, :], sl[:, 0, :], start=False, stop=True)
            mm(b[:, 2 * NE:3 * NE], ones[:, :], sl[:, 0, :], start=True, stop=False)
            close_bank(mm(b[:, 2 * NE:3 * NE], ones[:, :], sl[:, 1, :], start=False, stop=True), "cn")
            need(pe, "route_t", 1)
            b = open_bank(pe, "it")
            mm(b[:, 0:NITEM], ecol[:, 0:1].broadcast_to([P, P]), ident[:, 0:NITEM], start=True, stop=True)
            close_bank(mm(b[:, NITEM:2 * NITEM], ecol[:, 1:2].broadcast_to([P, P]), ident[:, 0:NITEM],
                          start=True, stop=True), "it")
            for i in range(4):
                need_sb(pe, f"ht{i // 2}{i % 2}")
            while turn[0] % 8:
                turn[0] += 1
            loop_fill["e"] = (list(fills), list(loads))
            f0 = list(fills)
            pe.wait_ge(S["tab_ready"], 2)
            items = pe.value_load(tab[0:1, NITEM:NITEM + 1], min_val=1, max_val=NITEM - 1)
            with pe.Fori(0, items) as i:
                use = {bi: 0 for bi in range(8)}
                PER = EPER

                def obank(bi):
                    pe.wait_ge(bank_done[bi], i * PER[bi] + f0[bi] + use[bi])
                    use[bi] += 1
                    return banks[bi]

                pe.wait_ge(S["sel_item"], i + 1)
                b = obank(4)
                for tt in range(NT):
                    ins = nc.tensor.transpose(b[:, tt * P:(tt + 1) * P], Sp[:, tt, :], ident[:, :])
                ins.then_inc(bank_full[4], 1)
                for g in range(2):
                    b = v4(obank(5 - g))
                    for j in range(4):
                        m = 4 * g + j
                        for tt in range(NT):
                            ins = mm(b[:, j, :], ht[:, tt, m * P:(m + 1) * P], Sl[:, tt, :],
                                     start=tt == 0, stop=tt == NT - 1)
                    ins.then_inc(bank_full[5 - g], 1)

                def slot_wait(n):
                    si, r = n % NSE, n // NSE
                    pe.wait_ge(slot_full[si], i * 48 + 16 * (loads[si] + r + 1))
                    return slots[si], si

                def up(j):
                    if j == 0:
                        pe.wait_ge(bank_done[5], i * PER[5] + f0[5] + 1)
                        pe.wait_ge(bank_done[4], i * PER[4] + f0[4] + 2)
                    for s in range(2):
                        t_, si = slot_wait(3 * j + s)
                        w = c3(t_, KD, 512)
                        bi = 2 * s + j % 2
                        b = obank(bi)
                        for k in range(KD):
                            ins = mm(b[:, :], xg[:, k, :], w[:, k, :], start=k == 0, stop=k == KD - 1)
                        ins.then_inc(bank_full[bi], 1)

                def down(j):
                    b2 = 2 + j % 2
                    pe.wait_ge(bank_done[b2], i * PER[b2] + f0[b2] + j // 2 + 1)
                    bi = 4 + j % 2
                    b = v4(obank(bi))
                    for k in range(4):
                        ins = nc.tensor.transpose(b[:, k, :], av[:, j % 2, k * P:(k + 1) * P], ident[:, :])
                    ins.then_inc(bank_full[bi], 1)

                def down2(j):
                    bi = 4 + j % 2
                    pe.wait_ge(bank_done[bi], i * PER[bi] + f0[bi] + use[bi])
                    t_, si = slot_wait(3 * j + 2)
                    w = c3(t_, 4, D)
                    for half in range(2):
                        if j == 0:
                            pe.wait_ge(bank_done[6 + half], i + f0[6 + half])
                        for k in range(4):
                            ins = mm(banks[6 + half][:, :], aT[:, j % 2, k, :], w[:, k, half * 512:half * 512 + 512],
                                     start=j == 0 and k == 0, stop=j == NJ - 1 and k == 3)
                    ins.then_inc(S["down_done"], 1)

                up(0)
                for j in range(NJ):
                    if j + 1 < NJ:
                        up(j + 1)
                    down(j)
                    down2(j)
                for half in range(2):
                    pe.wait_ge(bank_done[6 + half], i + f0[6 + half] + 1)
                for g in range(4):
                    b = v2(obank(g))
                    for j in range(2):
                        m = 2 * g + j
                        ins = mm(b[:, j, :], Ys[:, m * P:(m + 1) * P], SpT[:, :], start=True, stop=True)
                    ins.then_inc(bank_full[g], 1)
                assert use == {k: PER[k] for k in use} | {6: 0, 7: 0}, use

            n = 2 * DEPTH
            need(pe, "sq_ready", n + 1)
            for k in range(KD):
                ins = mm(banks[7][:, 0:T], ones[:, :], sq[:, k, :], start=k == 0, stop=k == KD - 1)
            ins.then_inc(S["y_item"], 1)
            need(pe, "h_ready", KD * (n + 1))
            for tt in range(NT):
                for g in range(2):
                    b = v4(banks[2 * tt + g])
                    for j in range(4):
                        k = 4 * g + j
                        ins = nc.tensor.transpose(b[:, j, :], h[:, k, tt * P:(tt + 1) * P], ident[:, :])
                    ins.then_inc(S["yscat"], 1)

        @block.sync
        def _(sp):
            def vec(tile, row, ap):
                n = ap.shape[0]
                sp.dma_start(rows[row:row + n, tile, :], ap).then_inc(S["rows_in"], 16)

            def lk(ap):
                return ap.rearrange("l (k p) -> (l k) p", p=P)

            sp.dma_start(xt[:, :, :], a["x"][0].rearrange("(t p) d -> p t d", p=P)).then_inc(S["x_in"], 16)
            vec(0, 0, lk(a["g_mix"]))
            vec(0, 16, lk(a["g_ffn"]))
            vec(0, 32, a["g_final"].rearrange("(k p) -> k p", p=P))
            vec(0, 40, a["dsa_kv_norm"])
            vec(0, 42, lk(a["rwkv_mu"]))
            vec(0, 70, lk(a["rwkv_w0"]))
            vec(0, 78, lk(a["rwkv_a0"]))
            vec(0, 86, lk(a["rwkv_k_k"]))
            vec(0, 94, lk(a["rwkv_k_a"]))
            vec(0, 102, a["rwkv_r_k"].rearrange("l (j u) c -> (l j) (u c)", u=2))
            vec(0, 110, lk(a["rwkv_ln_g"]))
            vec(0, 118, lk(a["rwkv_ln_b"]))
            vec(1, 0, lk(a["b_gate"]))
            vec(1, 48, lk(a["vres_v0"]))
            sp.dma_start(b_rt[:, :], a["router_b"]).then_inc(S["rows_in"], 16)

            def load(name, width, views):
                s, n = load_at[name]
                if (s, n - 1) in before:
                    sm, v = before[(s, n - 1)]
                    sp.wait_ge(sm, v)
                for i, (dst, src) in enumerate(views(slots[s])):
                    assert i == 0
                    sp.dma_start(dst, src).then_inc(slot_full[s], 16)

            before = {load_at[n]: released[n] for n in released}

            def columns(l, c0, n):
                src = w_in[l].rearrange("(k p) n -> p k n", p=P)[:, :, c0:c0 + n]
                return lambda t: [(c3(t, KD, n), src)]

            small = [
                (fbias[:, :], a["fox_f_bias"].rearrange("l h -> h l")),
                (vlmu[:, :], a["vres_mu"].rearrange("o c -> c o")),
                (w_lora[0:64, :, :], a["rwkv_w_up"].rearrange("l r c -> r l c")),
                (w_lora[64:128, :, :], a["rwkv_a_up"].rearrange("l r c -> r l c")),
                (g_lora[:, :, :], a["rwkv_g_up"].rearrange("l r c -> r l c")),
                (v_lora[:, :], a["vres_up"][0]),
                (v_down[:, :, :], a["vres_down"][0].rearrange("(k p) c -> p k c", p=P)),
                (w_uk[0:64, :, :, :], a["dsa_w_uk"].rearrange("l (g u) d r -> u d l g r", u=2)[0]),
                (w_uk[64:128, :, :, :], a["dsa_w_uk"].rearrange("l (g u) d r -> u d l g r", u=2)[1]),
                (w_uv[:, 0, :, :], a["dsa_w_uv"][0].rearrange("h r d -> r h d")),
                (w_uv[:, 1, :, :], a["dsa_w_uv"][1].rearrange("h r d -> r h d")),
                (w_rt[:, :, :], a["router_w"][0].rearrange("(k p) e -> p k e", p=P)),
            ]
            for l in range(DEPTH):
                L = f"{l}"
                load(L + "w0", 512, columns(l, FOX0, 512))
                load(L + "w1", 260, columns(l, FOX0 + 512, 260))
                load(L + "w2", 384, columns(l, DSA0, 384))
                if l == 0:
                    for dst, src in small:
                        sp.dma_start(dst, src, allow_slow_non_contiguous=True).then_inc(S["smallw_in"], 16)
                load(L + "w3", 296, columns(l, DSA0 + 384, 296))
                load(L + "w4", 512, columns(l, RW0, 512))
                load(L + "w5", 512, columns(l, RW0 + 512, 512))
                load(L + "w6", 512, columns(l, RW0 + 1024, 512))
                load(L + "w7", 256, columns(l, RW0 + 1536, 256))
                fl, ld, st0 = loop_fill[f"g{l}"]
                for s in range(3):
                    si = (st0 + s) % NS
                    sm, v = before[(si, ld[si])]
                    sp.wait_ge(sm, v)
                wv = w_in[l].rearrange("(k p) n -> p k n", p=P)
                with sp.Fori(0, GI) as i:
                    for s in range(3):
                        si = (st0 + s) % NS
                        src = wv[:, :, bass.ds(i * 1536 + (GATE0 + 512 * s), 512)]
                        bi = 2 * s + 1
                        sp.wait_ge(bank_full[bi], i + fl[bi])
                        sp.dma_start(c3(slots[si], KD, 512), src).then_inc(slot_full[si], 16)
                for s in range(3):
                    si = (st0 + s) % NS
                    before[(si, ld[si] + GI)] = (bank_full[2 * s + 1], fl[2 * s + 1] + GI)

                def branch(parts):
                    def views(t):
                        return parts(t)
                    return views

                s, n = load_at[L + "pa"]
                sm, v = before[(s, n - 1)]
                sp.wait_ge(sm, v)
                w = c3(slots[s], 4, D)
                sp.dma_start(w[:, 0:2, :], a["p_fox"][l].rearrange("(k p) n -> p k n", p=P)).then_inc(S["pa_half"], 16)
                sp.dma_start(w[:, 2:4, :], a["p_dsa"][l].rearrange("(k p) n -> p k n", p=P)).then_inc(slot_full[s], 16)
                load(L + "pb", 512, lambda t: [(c3(t, 4, D), a["p_rwkv"][l].rearrange("(k p) n -> p k n", p=P))])
                for s in range(2):
                    src = a["w_out"][l].rearrange("(k p) n -> p k n", p=P)[:, :, 512 * s:512 * s + 512]
                    load(f"{l}wo{s}", 512, lambda t: [(c3(t, KD, 512), src)])
                if l == 0:
                    fl, ld, st0 = loop_fill["d"]
                    sl3 = [(st0 + s) % NS for s in range(3)]
                    for si in sl3:
                        sm, v = before[(si, ld[si])]
                        sp.wait_ge(sm, v)
                    wg = a["ffn_w_gate"][0].rearrange("(k p) n -> p k n", p=P)
                    wu = a["ffn_w_up"][0].rearrange("(k p) n -> p k n", p=P)
                    wd = a["ffn_w_down"][0].rearrange("(k p) n -> p k n", p=P)
                    with sp.Fori(0, DI) as i:
                        srcs = [wg[:, :, bass.ds(i * 512, 512)], wu[:, :, bass.ds(i * 512, 512)],
                                wd[:, bass.ds(i * 4, 4), :]]
                        sp.wait_ge(bank_full[1], fl[1] + i)
                        sp.dma_start(c3(slots[sl3[0]], KD, 512), srcs[0]).then_inc(slot_full[sl3[0]], 16)
                        sp.wait_ge(bank_full[3], fl[3] + i)
                        sp.dma_start(c3(slots[sl3[1]], KD, 512), srcs[1]).then_inc(slot_full[sl3[1]], 16)
                        sp.wait_ge(S["down_done"], i)
                        sp.dma_start(c3(slots[sl3[2]], 4, D), srcs[2]).then_inc(slot_full[sl3[2]], 16)
                    c0 = DI * 512
                    sp.wait_ge(bank_full[1], fl[1] + DI)
                    sp.dma_start(c3(slots[sl3[0]], KD, 256), wg[:, :, c0:FF]).then_inc(slot_full[sl3[0]], 16)
                    sp.wait_ge(bank_full[3], fl[3] + DI)
                    sp.dma_start(c3(slots[sl3[1]], KD, 256), wu[:, :, c0:FF]).then_inc(slot_full[sl3[1]], 16)
                    sp.wait_ge(S["down_done"], DI)
                    sp.dma_start(c3(slots[sl3[2]], 2, D), wd[:, c0 // P:FF // P, :]).then_inc(slot_full[sl3[2]], 16)
                    before[(sl3[0], ld[sl3[0]] + DI + 1)] = (bank_full[0], fl[0] + DI + 1)
                    before[(sl3[1], ld[sl3[1]] + DI + 1)] = (bank_full[2], fl[2] + DI + 1)
                    before[(sl3[2], ld[sl3[2]] + DI + 1)] = (S["down_done"], DOWN0)
            for g in range(4):
                need_sb(sp, f"1xo{g}")
            sp.wait_ge(S["tab_ready"], 2)
            items = sp.value_load(tab[0:1, NITEM:NITEM + 1], min_val=1, max_val=NITEM - 1)
            f0, _ = loop_fill["e"]
            mg = a["moe_w_gate"][0].rearrange("e (k p) n -> e p k n", p=P)
            mu = a["moe_w_up"][0].rearrange("e (k p) n -> e p k n", p=P)
            md = a["moe_w_down"][0].rearrange("e (k p) n -> e p k n", p=P)
            with sp.Fori(0, items) as i:
                e = sp.value_load(tab[0:1, bass.ds(i, 1)], min_val=0, max_val=NE - 1)
                for n in range(3 * NJ):
                    j, kind = n // 3, n % 3
                    if kind < 2:
                        src = (mg, mu)[kind][bass.ds(e, 1), :, :, 512 * j:512 * j + 512].rearrange("o p k n -> (o p) k n")
                        dst = c3(slots[n % NSE], KD, 512)
                    else:
                        src = md[bass.ds(e, 1), :, 4 * j:4 * j + 4, :].rearrange("o p k n -> (o p) k n")
                        dst = c3(slots[n % NSE], 4, D)
                    q, back = (n - NSE, 0) if n >= NSE else (n - NSE + 3 * NJ, 1)
                    jq, kq = q // 3, q % 3
                    if kq < 2:
                        b = 2 * kq + jq % 2
                        sp.wait_ge(bank_full[b], i * EPER[b] + (f0[b] - back * EPER[b] + jq // 2 + 1))
                    else:
                        sp.wait_ge(S["down_done"], i * NJ + (DOWN0 - back * NJ + jq + 1))
                    sp.dma_start(dst, src).then_inc(slot_full[n % NSE], 16)
            sp.wait_ge(S["out_tok"], 4)
            sp.dma_start(out[0].rearrange("(t p) d -> p t d", p=P), xt[:, :, :]).then_inc(S["stored"], 16)
            sp.wait_ge(S["stored"], 16)

        @block.gpsimd
        def _(gp):
            count, sync = stepper(gp, "pool_step")

            def step(ins):
                count(ins)
                sync()
            sel = nc.gpsimd.affine_select
            step(nc.gpsimd.memset(ident[:, :], 0.0))
            step(nc.gpsimd.memset(ones[:, :], 1.0))
            step(nc.gpsimd.memset(blk[:, :], 0.0))
            step(nc.gpsimd.memset(upper[:, :, :], 1.0))
            step(nc.gpsimd.memset(level[:, :, :], 0.0))
            step(nc.gpsimd.memset(fmask[:, :, :], 0.0))
            step(nc.gpsimd.memset(dmask[:, :, :], 0.0))
            step(nc.gpsimd.memset(cst[:, 0:1], 0.0))
            step(nc.gpsimd.memset(cst[:, 1:2], EPS))
            step(nc.gpsimd.memset(cst[:, 2:3], 1e-12))
            step(nc.gpsimd.memset(cst[:, 3:4], LN_EPS))
            step(nc.gpsimd.memset(cst[:, 4:5], 1.0))
            step(nc.gpsimd.iota(iota_i[:, :], pattern=[[1, P]], base=0, channel_multiplier=0))
            step(nc.gpsimd.iota(pidx_i[:, :], pattern=[[0, 1]], base=0, channel_multiplier=1))
            sync()
            step(nc.gpsimd.tensor_copy(iota[:, :], iota_i[:, :]))
            step(nc.gpsimd.tensor_copy(pidx[:, :], pidx_i[:, :]))
            step(nc.gpsimd.memset(blk[0:64, 0:64], 1.0))
            step(nc.gpsimd.memset(blk[64:128, 64:128], 1.0))
            step(nc.gpsimd.memset(dmask[0:64, 0, 64:128], NEG))
            step(nc.gpsimd.memset(dmask[0:64, 1, 192:256], NEG))
            for lv in range(7):
                bs = 1 << lv
                step(nc.gpsimd.memset(level[:, lv, :].rearrange("p (n b) -> p n b", b=2 * bs)[:, :, bs:], 1.0))
            step(sel(out=ident[:, :], in_=ident[:, :], compare_op=ALU.not_equal, fill=1.0, base=0,
                     pattern=[[-1, P]], channel_multiplier=1))
            for q in range(4):
                step(sel(out=upper[:, q, :], in_=upper[:, q, :], compare_op=ALU.is_ge if q % 2 else ALU.is_gt,
                         fill=0.0, base=0, pattern=[[1, P]], channel_multiplier=-1))
            for qt in range(NT):
                o = fmask[:, qt, qt * P:(qt + 1) * P]
                step(sel(out=o, in_=o, compare_op=ALU.is_ge, fill=NEG, base=0, pattern=[[-1, P]],
                         channel_multiplier=1))
            sync()
            for lv in range(7):
                bs = 1 << lv
                o = level[:, lv, :].rearrange("p (n b) -> p n b", b=2 * bs)[:, :, bs:]
                step(sel(out=o, in_=o, compare_op=ALU.is_ge, fill=0.0, base=0,
                         pattern=[[-2 * bs, P // (2 * bs)], [0, bs]], channel_multiplier=1))
            sync()
            for lv in range(7):
                bs = 1 << lv
                o = level[:, lv, :].rearrange("p (n b) -> p n b", b=2 * bs)[:, :, bs:]
                step(sel(out=o, in_=o, compare_op=ALU.is_ge, fill=0.0, base=bs - 1,
                         pattern=[[2 * bs, P // (2 * bs)], [0, bs]], channel_multiplier=-1))
            sync()
            nc.gpsimd.memset(cst[:, 5:6], 0.0).then_inc(S["consts"], 1)
            for l in range(DEPTH):
                s_, n_ = load_at[f"{l}w3"]
                gp.wait_ge(slot_full[s_], 16 * n_)
                src = c3(slots[s_], KD, 296)[:, :, 256:288]
                for q in range(4):
                    ins = nc.gpsimd.tensor_copy(wrep[:, :, 32 * q:32 * q + 32], src)
                    if q < 3:
                        step(ins)
                ins.then_inc(S["ik_w"], 1)
                need(gp, "ar_ready", l + 1)
                need_sb(gp, f"{l}vt1")
                need_sb(gp, f"{l}bo1")
                for lev in range(7):
                    for g in range(4):
                        if lev == 0:
                            for m in range(4 * g, 4 * g + 4):
                                need_sb(gp, f"{l}B{m}")
                        elif lev == 1:
                            need_sb(gp, f"{l}x0{g}")
                        else:
                            take(gp, f"{l}x{lev - 1}{g}")
                        nc.gpsimd.tensor_tensor(Lo[:, 4 * g:4 * g + 4, :], Bm[:, 4 * g:4 * g + 4, 0, :],
                                                level[:, lev:lev + 1, :].broadcast_to([P, 4, P]),
                                                ALU.mult).then_inc(S["lo_ready"], 1)

        @block.scalar
        def _(act):
            A = nc.scalar.activation
            step, sync = stepper(act, "scalar_step")
            need(act, "consts", 1)
            need(act, "smallw_in", 16 * 12)

            def copy(o, i, scale=1.0):
                return A(o, i, ACT.Copy, scale=scale)

            def evac(name, o, sel=lambda b: b[:, :], scale=1.0):
                b = take(act, name)
                done(copy(o, sel(b), scale), name)

            def norm_sq(n):
                need(act, "x_ready", n + 1)
                A(sq[:, :, :], x[:, :, :], ACT.Square, scale=1 / 32).then_inc(S["sq_ready"], 1)

            def norm_std(n):
                b = take(act, f"ss{n}")
                done(A(rs[:, :], b[:, 0:T], ACT.Sqrt, bias=cst[:, 1:2]), f"ss{n}")

            def exps(n, l):
                for part, buf in enumerate((L0, L1b)):
                    need(act, "max_ready", 2 * n + part + 1)
                    for hh in range(4):
                        A(buf[:, hh, :], buf[:, hh, :], ACT.Exp, bias=st[:, 2 * (n % 2) + part, 1, hh:hh + 1],
                          scale=0.125, accum_out=st[:, 2 * (n % 2) + part, 2, hh:hh + 1]
                          ).then_inc(S["exp_ready"], 1)

            for l in range(DEPTH):
                L = f"{l}"
                norm_sq(2 * l)
                norm_std(2 * l)
                evac(L + "fq", fq[:, :, :], v2)
                evac(L + "fk", fk[:, :, :], v2)
                evac(L + "fv", fv[:, :, :], v2)
                b = take(act, L + "ff")
                done(A(fz[:, :], b[0:4, 0:T], ACT.Identity, bias=fbias[:, l:l + 1]), L + "ff")
                b = take(act, L + "cc")
                step(A(cc[:, :], b[:, 0:T], ACT.Copy))
                A(ccs[:, :], b[:, 0:T], ACT.Square, scale=KV ** -0.5).then_inc(S["css"], 1)
                need(act, "css", l + 1)
                done(A(ccs[0:1, 0:1], ccs[0:1, 0:1], ACT.Copy), L + "cc")
                evac(L + "dq", dq[:, :, :], v2)
                evac(L + "iq", iq[:, :, :], v2)
                evac(L + "ik", ik[:, :], lambda b: b[:, 0:T])
                evac(L + "iw", iw[:, :, :], lambda b: b[:, 0:2 * IH].rearrange("p (t e) -> p t e", t=2), 1 / 16)
                need(act, "fox_z", l + 1)
                A(ft[:, :], ft[:, :], ACT.Exp, scale=-1.0).then_inc(S["fox_e"], 1)
                need(act, "fox_e", l + 1)
                A(ft[:, :], ft[:, :], ACT.Ln, bias=cst[0:4, 4:5]).then_inc(S["fox_l"], 1)
                for i in range(8):
                    n = f"{l}rel{i // 4}{i % 4}"
                    b = take(act, n)
                    if 8 * l + i >= 2:
                        need(act, "rel_used", 8 * l + i - 1)
                    w = 2 * P * (i // 4 + 1)
                    done(A(rel[:, i % 2, 0:w], b[:, 0:w], ACT.Relu), n)
                b = take(act, L + "css")
                done(A(crin[:, :], b[:, 0:T], ACT.Sqrt, bias=cst[:, 1:2]), L + "css")
                evac(L + "ql0", ql[:, 0:4:2, :], v2)
                evac(L + "ql1", ql[:, 1:4:2, :], v2)
                evac(L + "r0", raw[:, 0:2, 1:], v2)
                evac(L + "r1", raw[:, 2:4, 1:], v2)
                exps(2 * l, l)
                evac(L + "k0", raw[:, 4:6, 1:], v2)
                evac(L + "k1", raw[:, 6:8, 1:], v2)
                evac(f"{l}ft0", PT0[:, :, 0:P], v4)
                evac(f"{l}ft1", PT0[:, :, P:T], v4)
                evac(f"{l}ft2", PT1[:, :, :], v4)
                evac(L + "v0", raw[:, 8:10, 1:], v2)
                evac(L + "fo", oF[:, :, :], v2)
                evac(L + "v1", raw[:, 10:12, 1:], v2)
                evac(L + "wg", raw[:, 12:14, 1:], v2)
                if l:
                    evac(L + "vl", raw[0:32, 14, 1:], lambda b: b[0:32, 0:T])
                evac(L + "ct", ct[:, :, :], lambda b: v2(b)[:, 0, :].rearrange("p (t q) -> p t q", t=2))
                exps(2 * l + 1, l)
                evac(f"{l}dt0", PT0[:, :, 0:P], v4)
                evac(f"{l}dt1", PT0[:, :, P:T], v4)
                evac(f"{l}dt2", PT1[:, :, :], v4)
                evac(L + "ol0", ol[:, 0:2, :], v2)
                evac(L + "ol1", ol[:, 2:4, :], v2)
                evac(L + "do", oD[:, :, :], v2)
                need(act, "shift_ready", 2 * l + 1)
                A(mx[0:64, 12, :], mx[0:64, 12, :], ACT.Tanh).then_inc(S["tanh_ready"], 1)
                A(mx[:, 13, :], mx[:, 13, :], ACT.Sigmoid).then_inc(S["tanh_ready"], 1)
                for nm, o, v0 in (("zw", sg, 70), ("za", aa, 78)):
                    for g in range(2):
                        b = v2(take(act, f"{l}{nm}{g}"))
                        step(A(o[:, 2 * g, :], b[:, 0, :], ACT.Sigmoid, bias=VA[:, v0 + 4 * l + 2 * g:v0 + 4 * l + 2 * g + 1]))
                        done(A(o[:, 2 * g + 1, :], b[:, 1, :], ACT.Sigmoid,
                               bias=VA[:, v0 + 4 * l + 2 * g + 1:v0 + 4 * l + 2 * g + 2]), f"{l}{nm}{g}")
                for g in range(2):
                    evac(f"{l}zg{g}", gg[:, 2 * g:2 * g + 2, :], v2)
                if l:
                    for g in range(2):
                        b = v2(take(act, f"{l}zv{g}"))
                        step(A(kp[:, 2 * g, :], b[:, 0, :], ACT.Sigmoid, bias=VB[:, 48 + 2 * g:49 + 2 * g]))
                        done(A(kp[:, 2 * g + 1, :], b[:, 1, :], ACT.Sigmoid, bias=VB[:, 49 + 2 * g:50 + 2 * g]),
                             f"{l}zv{g}")
                for g in range(2):
                    b = take(act, f"{l}ks{g}")
                    done(A(kstd[:, 2 * g:2 * g + 2, :], v2(b), ACT.Sqrt, bias=cst[:, 2:3]), f"{l}ks{g}")
                evac(f"{l}vt0", vt[:, 0, :])
                evac(f"{l}vt1", vt[:, 1, :])
                need(act, "cum_ready", l + 1)
                need(act, "kk_ready", l + 1)
                for j in range(4):
                    for c in range(2):
                        step(A(ep[:, j, c, :], cum[:, j, c, :], ACT.Exp, scale=-DECAY, bias=fac[:, j, c:c + 1]))
                        step(A(em[:, j, c, :], cum[:, j, c, 1:], ACT.Exp, scale=DECAY, bias=fac[:, j, 2 + c:3 + c]))
                A(zf[:, :], zf[:, :], ACT.Exp, scale=-DECAY).then_inc(S["exps_ready"], 1)
                evac(L + "bt", bt[:, :])
                evac(L + "kt", kt[:, :])
                for lev in range(1, 7):
                    for g in range(4):
                        evac(f"{l}x{lev}{g}", Xs[:, 4 * g:4 * g + 4, :], v4)
                for c in range(2):
                    for odd in range(2):
                        evac(f"{l}G{c}{odd}", Gs[:, :].rearrange("p (j u v) -> p u j v", u=2, v=HD)[:, odd],
                             lambda b: b[:, 0:256].rearrange("p (j v) -> p j v", v=HD))
                    evac(f"{l}SA{c}", SA[:, :])
                for g in range(2):
                    need_sb(act, f"{l}gm{g}")
                    A(ysq[:, 2 * g:2 * g + 2, :], ym[:, 2 * g:2 * g + 2, :], ACT.Square, scale=0.125).then_inc(S["gsq"], 1)
                for g in range(2):
                    b = take(act, f"{l}gv{g}")
                    done(A(ysq[:, 2 * g:2 * g + 2, :], v2(b), ACT.Sqrt, bias=cst[:, 3:4]), f"{l}gv{g}")
                fl, _, _ = loop_fill[f"g{l}"]
                with act.Fori(0, GI) as i:
                    for bi in range(6):
                        act.wait_ge(bank_full[bi], i + (fl[bi] + 1))
                        b = v2(banks[bi])
                        for j in range(2):
                            m = i * 12 + (2 * bi + j)
                            ins = A(gates[:, bass.ds(m, 1), :].rearrange("p o t -> p (o t)"), b[:, j, :], ACT.Sigmoid,
                                    bias=VB[:, bass.ds(m + 24 * l, 1)])
                        ins.then_inc(bank_done[bi], 1)
                norm_sq(2 * l + 1)
                norm_std(2 * l + 1)
                if l == 0:
                    fl, _, _ = loop_fill["d"]

                    def silu(i, nf):
                        for g in range(nf // 2):
                            act.wait_ge(bank_full[g], i + (fl[g] + 1))
                            act.wait_ge(bank_done[2 + g], i + fl[2 + g])
                            A(hsig[:, 2 * g:2 * g + 2, :], v2(banks[g]), ACT.Silu).then_inc(bank_done[g], 1)
                    with act.Fori(0, DI) as i:
                        silu(i, 4)
                    silu(DI, 2)
            need(act, "route", 1)
            for tt in range(NT):
                ins = A(ex[:, tt, :], lg[:, tt, :], ACT.Exp, bias=nr[:, tt:tt + 1])
                ins.then_inc(S["route_e"], 1)
            for tt in range(NT):
                for g in range(2):
                    evac(f"ht{tt}{g}", ht[:, tt, 512 * g:512 * g + 512])
            f0, _ = loop_fill["e"]
            act.wait_ge(S["tab_ready"], 2)
            items = act.value_load(tab[0:1, NITEM:NITEM + 1], min_val=1, max_val=NITEM - 1)
            with act.Fori(0, items) as i:
                def full(bi, r):
                    act.wait_ge(bank_full[bi], i * EPER[bi] + (f0[bi] + r + 1))
                    return banks[bi]

                A(SpT[:, :], full(4, 0)[:, 0:T], ACT.Copy).then_inc(bank_done[4], 1)

                def silu(j):
                    b = full(j % 2, j // 2)
                    act.wait_ge(bank_done[2 + j % 2], i * EPER[2 + j % 2] + (f0[2 + j % 2] + j // 2))
                    A(gs[:, j % 2, :], b[:, :], ACT.Silu).then_inc(bank_done[j % 2], 1)
                silu(0)
                for j in range(NJ):
                    if j + 1 < NJ:
                        silu(j + 1)
                    bi = 4 + j % 2
                    b = full(bi, 2 + j // 2 if bi == 4 else 1 + j // 2)
                    A(aT[:, j % 2, :, :], v4(b), ACT.Copy).then_inc(bank_done[bi], 1)
                act.wait_ge(S["down_done"], i * NJ + (DOWN0 + NJ))
                A(Ys[:, 0:512], banks[6][:, :], ACT.Copy).then_inc(bank_done[6], 1)
            n = 2 * DEPTH
            need(act, "x_final", 1)
            A(sq[:, :, :], x[:, :, :], ACT.Square, scale=1 / 32).then_inc(S["sq_ready"], 1)
            need(act, "y_item", 1)
            A(rs[:, :], banks[7][:, 0:T], ACT.Sqrt, bias=cst[:, 1:2]).then_inc(S["fin_ready"], 1)
            for tt in range(NT):
                need(act, "yscat", 2 * tt + 1)
                A(xt[:, tt, 0:512], banks[2 * tt][:, :], ACT.Copy).then_inc(S["out_tok"], 1)

        @block.vector
        def _(dve):
            V = nc.vector
            tt_ = V.tensor_tensor
            step, sync = stepper(dve, "vector_step")

            def col(t, c):
                return t[:, c:c + 1]

            b = take(dve, "vecs")
            step(V.tensor_copy(VA[:, 0:126], b[:, 0:126]))
            done(V.tensor_copy(VB[:, 0:52], b[:, 128:180]), "vecs")
            for t in range(NT):
                for g in range(2):
                    n = f"x{t}{g}"
                    b = v4(take(dve, n))
                    done(V.tensor_copy(x[:, 4 * g:4 * g + 4, t * P:(t + 1) * P], b), n)
            for t in range(NT):
                for g in range(2):
                    need_sb(dve, f"x{t}{g}")
            need(dve, "consts", 1)
            need(dve, "smallw_in", 16 * 12)
            V.memset(cst[:, 6:7], 0.0).then_inc(S["x_ready"], 1)

            def norm(n, g0):
                need_sb(dve, f"ss{n}")
                step(V.reciprocal(rs[:, :], rs[:, :]))
                sync()
                for k in range(KD):
                    V.scalar_tensor_tensor(out=h[:, k, :], in0=x[:, k, :], scalar=col(VA, g0 + k), in1=rs[:, :],
                                           op0=ALU.mult, op1=ALU.mult).then_inc(S["h_ready"], 1)

            def scores(l, nm, n, mask):
                for part, (buf, nk) in enumerate(((L0, P), (L1b, T))):
                    s_ = st[:, 2 * (n % 2) + part]
                    m = mask[:, part:part + 1, 0:nk]
                    for odd in range(2):
                        name = f"{l}{nm}l{2 * part + odd}"
                        b = v2(take(dve, name))
                        done(tt_(buf[:, odd:4:2, :], b[:, :, 0:nk], m.broadcast_to([P, 2, nk]), ALU.add), name)
                    need_sb(dve, f"{l}{nm}l{2 * part}")
                    need_sb(dve, f"{l}{nm}l{2 * part + 1}")
                    step(V.tensor_reduce(out=s_[:, 0, :], in_=buf[:, :, :], op=ALU.max, axis=AX))
                    sync()
                    V.tensor_scalar(s_[:, 1, :], s_[:, 0, :], -0.125, None, ALU.mult).then_inc(S["max_ready"], 1)
                for part, (buf, nk) in enumerate(((L0, P), (L1b, T))):
                    s_ = st[:, 2 * (n % 2) + part]
                    need(dve, "exp_ready", 8 * n + 4 * part + 4)
                    step(V.reciprocal(s_[:, 3, :], s_[:, 2, :]))
                    sync()
                    tt_(buf[:, :, :], buf[:, :, :], s_[:, 3, :].unsqueeze(2).broadcast_to([P, 4, nk]),
                        ALU.mult).then_inc(S["p_ready"], 1)

            for l in range(DEPTH):
                L = f"{l}"
                norm(2 * l, 8 * l)
                step(V.memset(raw[:, :, 0:1], 0.0))
                need_sb(dve, L + "ff")
                V.scalar_tensor_tensor(out=ft[:, :], in0=fz[:, :], scalar=-1.0, in1=fz[:, :], op0=ALU.mult,
                                       op1=ALU.max).then_inc(S["fox_z"], 1)
                need(dve, "fox_l", l + 1)
                step(V.scalar_tensor_tensor(out=fz[:, :], in0=fz[:, :], scalar=0.0, in1=ft[:, :],
                                            op0=ALU.min, op1=ALU.subtract))
                sync()
                step(V.tensor_tensor_scan(F8[:, :], fz[:, :], fz[:, :], 0.0, ALU.add, ALU.min))
                sync()
                step(V.tensor_scalar(nF8[:, :], F8[:, :], -8.0, None, ALU.mult))
                V.tensor_scalar(F8[:, :], F8[:, :], 8.0, None, ALU.mult).then_inc(S["fox_F"], 1)
                need_sb(dve, L + "iw")
                for i in range(8):
                    qt = i // 4
                    nk = P * (qt + 1)
                    need_sb(dve, f"{l}rel{qt}{i % 4}")
                    for j in range(2):
                        hh = i % 4 + 4 * j
                        r_ = rel[:, i % 2, j * nk:(j + 1) * nk]
                        o = sc[:, qt, 0:nk]
                        if hh == 0:
                            ins = V.tensor_scalar(o, r_, iw[:, qt, hh:hh + 1], None, ALU.mult)
                        else:
                            sync()
                            ins = V.scalar_tensor_tensor(out=o, in0=r_, scalar=iw[:, qt, hh:hh + 1], in1=o,
                                                         op0=ALU.mult, op1=ALU.add)
                        if j == 1:
                            ins.then_inc(S["rel_used"], 1)
                            need(dve, "rel_used", 8 * l + i + 1)
                        else:
                            step(ins)
                need_sb(dve, L + "css")
                need_sb(dve, L + "cc")
                step(V.reciprocal(crin[:, :], crin[:, :]))
                sync()
                V.scalar_tensor_tensor(out=cn[:, :], in0=cc[:, :], scalar=col(VA, 40 + l), in1=crin[:, :],
                                       op0=ALU.mult, op1=ALU.mult).then_inc(S["cn_ready"], 1)
                scores(l, "f", 2 * l, fmask)
                nks = (P, T)
                for qt in range(NT):
                    step(tt_(sc[:, qt, 0:nks[qt]], sc[:, qt, 0:nks[qt]], dmask[:, qt, 0:nks[qt]], ALU.add))
                sync()
                for r in range(TOPK // 8):
                    for qt in range(NT):
                        src = (sc if r == 0 else wk)[:, qt, 0:nks[qt]]
                        step(V.max(m8[:, qt, :], src))
                    sync()
                    if r < TOPK // 8 - 1:
                        for qt in range(NT):
                            src = (sc if r == 0 else wk)[:, qt, 0:nks[qt]]
                            step(V.match_replace(wk[:, qt, 0:nks[qt]], m8[:, qt, :], src, -3e38))
                        sync()
                for qt in range(NT):
                    s_, k_ = sc[:, qt, 0:nks[qt]], wk[:, qt, 0:nks[qt]]
                    step(V.tensor_scalar(k_, s_, m8[:, qt, 7:8], None, ALU.is_gt))
                    step(V.tensor_scalar(eq[:, qt, 0:nks[qt]], s_, m8[:, qt, 7:8], None, ALU.is_equal))
                sync()
                for qt in range(NT):
                    e_ = eq[:, qt, 0:nks[qt]]
                    step(V.tensor_reduce(out=cnt[:, qt:qt + 1], in_=wk[:, qt, 0:nks[qt]], op=ALU.add, axis=AX))
                    step(V.tensor_tensor_scan(cs[:, qt, 0:nks[qt]], e_, e_, 0.0, ALU.add, ALU.max))
                sync()
                step(V.tensor_scalar(cnt[:, :], cnt[:, :], -1.0, float(TOPK), ALU.mult, ALU.add))
                sync()
                for qt in range(NT):
                    e_ = eq[:, qt, 0:nks[qt]]
                    step(V.scalar_tensor_tensor(out=e_, in0=cs[:, qt, 0:nks[qt]], scalar=cnt[:, qt:qt + 1],
                                                in1=e_, op0=ALU.is_le, op1=ALU.mult))
                sync()
                for qt in range(NT):
                    k_ = wk[:, qt, 0:nks[qt]]
                    step(tt_(k_, k_, eq[:, qt, 0:nks[qt]], ALU.add))
                sync()
                for qt in range(NT):
                    k_ = wk[:, qt, 0:nks[qt]]
                    step(V.tensor_scalar(k_, k_, 1.0, -NEG, ALU.subtract, ALU.mult))
                sync()
                scores(l, "d", 2 * l + 1, wk)

                def shift(t0, t1, last=None):
                    step(tt_(mx[:, t0:t1, :], raw[:, t0:t1, 0:T], raw[:, t0:t1, 1:], ALU.subtract))
                    sync()
                    for t in range(t0, t1):
                        ins = V.scalar_tensor_tensor(out=mx[:, t, :], in0=mx[:, t, :], scalar=col(VA, 42 + 14 * l + t),
                                                     in1=raw[:, t, 1:], op0=ALU.mult, op1=ALU.add)
                        if last and t == t1 - 1:
                            ins.then_inc(S[last], 1)
                        else:
                            step(ins)
                need_sb(dve, L + "wg")
                shift(12, 14, "shift_ready")
                need(dve, "shift_ready", 2 * l + 1)
                if l:
                    need_sb(dve, L + "vl")
                    step(tt_(vl[:, :], raw[0:32, 14, 0:T], raw[0:32, 14, 1:], ALU.subtract))
                    sync()
                    V.scalar_tensor_tensor(out=vl[:, :], in0=vl[:, :], scalar=vlmu[:, 0:1], in1=raw[0:32, 14, 1:],
                                           op0=ALU.mult, op1=ALU.add).then_inc(S["shift_ready"], 1)
                else:
                    V.memset(cst[:, 7:8], 0.0).then_inc(S["shift_ready"], 1)
                need_sb(dve, L + "v1")
                shift(4, 8)
                shift(8, 12)
                shift(0, 4)
                sync()
                for j in range(4):
                    step(V.tensor_scalar(kk[:, j, :], mx[:, 4 + j, :], col(VA, 86 + 4 * l + j), None, ALU.mult))
                sync()
                tt_(bb[:, :, :], kk[:, :, :], kk[:, :, :], ALU.mult).then_inc(S["kks"], 1)
                if l == 0:
                    step(V.tensor_copy(vf[:, :, :], mx[:, 8:12, :]))
                    V.memset(cst[:, 7:8], 0.0).then_inc(S["v_ready"], 1)
                else:
                    need_sb(dve, L + "zv0")
                    need_sb(dve, L + "zv1")
                    step(tt_(vf[:, :, :], vf[:, :, :], mx[:, 8:12, :], ALU.subtract))
                    sync()
                    step(tt_(vf[:, :, :], vf[:, :, :], kp[:, :, :], ALU.mult))
                    sync()
                    tt_(mx[:, 8:12, :], mx[:, 8:12, :], vf[:, :, :], ALU.add).then_inc(S["v_ready"], 1)
                    need(dve, "v_ready", l + 1)
                need_sb(dve, L + "zw0")
                need_sb(dve, L + "zw1")
                step(V.memset(cum[:, :, :, 0:1], 0.0))
                for j in range(4):
                    for c in range(2):
                        s_ = sg[:, j, c * P:(c + 1) * P]
                        step(V.tensor_tensor_scan(cum[:, j, c, 1:], s_, s_, 0.0, ALU.add, ALU.max))
                sync()
                mid = P // 2
                step(V.tensor_scalar(fac[:, :, 0:2], cum[:, :, :, mid], DECAY, None, ALU.mult))
                step(V.tensor_scalar(fac[:, :, 2:4], cum[:, :, :, mid], -DECAY, None, ALU.mult))
                step(tt_(zf[:, :], cum[:, :, 0, P], cum[:, :, 0, mid], ALU.subtract))
                sync()
                tt_(zf[:, :], zf[:, :], cum[:, :, 1, mid], ALU.add).then_inc(S["cum_ready"], 1)
                need_sb(dve, L + "ks0")
                need_sb(dve, L + "ks1")
                step(V.reciprocal(kstd[:, :, :], kstd[:, :, :]))
                sync()
                tt_(kk[:, :, :], kk[:, :, :], kstd[:, :, :], ALU.mult).then_inc(S["kk_ready"], 1)
                need(dve, "kk_ready", l + 1)
                need_sb(dve, L + "za0")
                need_sb(dve, L + "za1")
                for j in range(4):
                    step(V.tensor_scalar(kp[:, j, :], aa[:, j, :], 1.0, col(VA, 94 + 4 * l + j), ALU.subtract, ALU.mult))
                step(tt_(bb[:, :, :], kk[:, :, :], aa[:, :, :], ALU.mult))
                sync()
                step(V.scalar_tensor_tensor(out=kp[:, :, :], in0=kp[:, :, :], scalar=1.0, in1=mx[:, 4:8, :],
                                            op0=ALU.add, op1=ALU.mult))
                sync()
                for j in range(4):
                    ins = V.scalar_tensor_tensor(out=aa[:, j, :], in0=mx[:, j, :], scalar=col(VA, 102 + 4 * l + j),
                                                 in1=kp[:, j, :], op0=ALU.mult, op1=ALU.mult)
                    if j < 3:
                        step(ins)
                ins.then_inc(S["rk_ready"], 1)
                need(dve, "exps_ready", l + 1)

                def hc(t):
                    return t.rearrange("p j (c t) -> p j c t", c=2)
                step(V.scalar_tensor_tensor(out=AR[:, :, :, 0, :], in0=hc(kk[:, :, :]), scalar=-1.0, in1=ep[:, :, :, 0:P],
                                            op0=ALU.mult, op1=ALU.mult))
                step(tt_(AR[:, :, :, 1, :], hc(mx[:, 0:4, :]), ep[:, :, :, 1:], ALU.mult))
                step(tt_(BK[:, :, :, 0, :], hc(bb[:, :, :]), em[:, :, :, :], ALU.mult))
                tt_(BK[:, :, :, 1, :], hc(kp[:, :, :]), em[:, :, :, :], ALU.mult).then_inc(S["ar_ready"], 1)
                for g in range(2):
                    b = v2(take(dve, f"{l}bo{g}"))
                    done(tt_(bon[:, 2 * g:2 * g + 2, :], b, mx[:, 8 + 2 * g:10 + 2 * g, :], ALU.mult), f"{l}bo{g}")
                for m in range(16):
                    b = v4(take(dve, f"{l}B{m}"))
                    done(tt_(Bm[:, m, :, :], b, upper[:, :, :], ALU.mult), f"{l}B{m}")
                idb = ident[:, :].unsqueeze(1).broadcast_to([P, 4, P])
                for g in range(4):
                    gsl = slice(4 * g, 4 * g + 4)
                    need(dve, "lo_ready", 28 * l + g + 1)
                    step(tt_(Tt[:, gsl, :], Lo[:, gsl, :], idb, ALU.add))
                    b = v4(take(dve, f"{l}x0{g}"))
                    done(tt_(Ti[:, gsl, :], b, idb, ALU.add), f"{l}x0{g}")
                for lev in range(1, 7):
                    for g in range(4):
                        gsl = slice(4 * g, 4 * g + 4)
                        prev = "x" if lev == 1 else "z"
                        need_sb(dve, f"{l}{prev}{lev - 1}{g}")
                        if lev < 6:
                            b = v4(take(dve, f"{l}y{lev}{g}"))
                            done(tt_(Ti[:, gsl, :], Ti[:, gsl, :], b, ALU.add), f"{l}y{lev}{g}")
                        b = v4(take(dve, f"{l}z{lev}{g}"))
                        done(tt_(Tt[:, gsl, :], Tt[:, gsl, :], b, ALU.add), f"{l}z{lev}{g}")
                b = take(dve, L + "Z")
                done(tt_(Zs[:, :, :], b[:, 0:256].rearrange("p (j v) -> p j v", j=4),
                         zf[:, :].unsqueeze(2).broadcast_to([P, 4, HD]), ALU.mult), L + "Z")
                for c in range(2):
                    b = v4(take(dve, f"{l}Y{c}"))
                    done(V.tensor_copy(yT[:, :, c * P:(c + 1) * P], b), f"{l}Y{c}")
                need_sb(dve, f"{l}Y0")
                need_sb(dve, f"{l}Y1")
                for g in range(2):
                    gsl = slice(2 * g, 2 * g + 2)
                    b = v2(take(dve, f"{l}gm{g}"))
                    done(V.scalar_tensor_tensor(out=ym[:, gsl, :], in0=b, scalar=-1.0 / HD, in1=yT[:, gsl, :],
                                                op0=ALU.mult, op1=ALU.add), f"{l}gm{g}")
                need_sb(dve, f"{l}gm0")
                need_sb(dve, f"{l}gm1")
                for g in range(2):
                    gsl = slice(2 * g, 2 * g + 2)
                    need_sb(dve, f"{l}gv{g}")
                    step(V.reciprocal(ysq[:, gsl, :], ysq[:, gsl, :]))
                sync()
                step(tt_(yT[:, :, :], ym[:, :, :], ysq[:, :, :], ALU.mult))
                sync()
                for j in range(4):
                    step(V.tensor_scalar(yT[:, j, :], yT[:, j, :], col(VA, 110 + 4 * l + j), col(VA, 118 + 4 * l + j),
                                         ALU.mult, ALU.add))
                sync()
                need_sb(dve, f"{l}bo0")
                need_sb(dve, f"{l}bo1")
                step(tt_(yT[:, :, :], yT[:, :, :], bon, ALU.add))
                sync()
                tt_(yT[:, :, :], yT[:, :, :], gg, ALU.mult).then_inc(S["o_ready"], 1)
                fl, _, _ = loop_fill[f"g{l}"]
                for bi in range(6):
                    dve.wait_ge(bank_done[bi], fl[bi] + GI)
                need(dve, "o_ready", l + 1)
                for i, nm in enumerate(("pf", "pd", "pr")):
                    for g in range(4):
                        b = v2(take(dve, f"{l}{nm}{g}"))
                        gt_ = gates[:, 8 * i + 2 * g:8 * i + 2 * g + 2, :]
                        o = sq[:, 2 * g:2 * g + 2, :]
                        if i == 0:
                            done(tt_(o, b, gt_, ALU.mult), f"{l}{nm}{g}")
                        else:
                            done(tt_(mtmp[:, g, :, :], b, gt_, ALU.mult), f"{l}{nm}{g}")
                    if i:
                        for g in range(4):
                            need_sb(dve, f"{l}{nm}{g}")
                            if i == 1:
                                need_sb(dve, f"{l}pf{g}")
                            o = sq[:, 2 * g:2 * g + 2, :]
                            ins = tt_(o, o, mtmp[:, g, :, :], ALU.add)
                            if i == 1:
                                step(ins)
                            else:
                                ins.then_inc(S["merged"], 1)
                        if i == 1:
                            sync()
                for g in range(4):
                    b = v2(take(dve, f"{l}xo{g}"))
                    o = x[:, 2 * g:2 * g + 2, :]
                    done(tt_(o, o, b, ALU.add), f"{l}xo{g}")
                for g in range(4):
                    need_sb(dve, f"{l}xo{g}")
                V.memset(cst[:, 6:7], 0.0).then_inc(S["x_ready"], 1)
                norm(2 * l + 1, 16 + 8 * l)
                if l == 0:
                    fl, _, _ = loop_fill["d"]

                    def hidden(i, nf):
                        for g in range(nf // 2):
                            dve.wait_ge(bank_full[2 + g], i + (fl[2 + g] + 1))
                            dve.wait_ge(bank_done[g], i + (fl[g] + 1))
                            tt_(hid[:, 2 * g:2 * g + 2, :], hsig[:, 2 * g:2 * g + 2, :], v2(banks[2 + g]),
                                ALU.mult).then_inc(bank_done[2 + g], 1)
                    with dve.Fori(0, DI) as i:
                        hidden(i, 4)
                    hidden(DI, 2)
                    need(dve, "down_done", DOWN0)
                    for g in range(4):
                        o = x[:, 2 * g:2 * g + 2, :]
                        tt_(o, o, v2(banks[4 + g]), ALU.add).then_inc(bank_done[4 + g], 1)
                    for g in range(4):
                        dve.wait_ge(bank_done[4 + g], fl[4 + g] + 1)
                    V.memset(cst[:, 6:7], 0.0).then_inc(S["x_ready"], 1)

            b = take(dve, "rt")
            done(V.tensor_copy(lg[:, :, :], b[:, 0:2 * NE].rearrange("p (t e) -> p t e", t=2)), "rt")
            need_sb(dve, "rt")
            for t in range(NT):
                step(V.max(mr[:, t, :], lg[:, t, :]))
            sync()
            V.tensor_scalar(nr[:, 0:2], mr[:, :, 0], -1.0, None, ALU.mult).then_inc(S["route"], 1)
            for t in range(NT):
                step(V.tensor_scalar(sl[:, t, :], lg[:, t, :], mr[:, t, 1:2], None, ALU.is_gt))
                step(V.tensor_scalar(eqr[:, t, :], lg[:, t, :], mr[:, t, 1:2], None, ALU.is_equal))
            sync()
            step(V.tensor_reduce(out=nr[:, 2:4], in_=sl[:, :, :], op=ALU.add, axis=AX))
            for t in range(NT):
                step(V.tensor_tensor_scan(csr[:, t, :], eqr[:, t, :], eqr[:, t, :], 0.0, ALU.add, ALU.max))
            sync()
            step(V.tensor_scalar(nr[:, 2:4], nr[:, 2:4], -1.0, 2.0, ALU.mult, ALU.add))
            sync()
            for t in range(NT):
                step(V.scalar_tensor_tensor(out=eqr[:, t, :], in0=csr[:, t, :], scalar=nr[:, 2 + t:3 + t],
                                            in1=eqr[:, t, :], op0=ALU.is_le, op1=ALU.mult))
            sync()
            tt_(sl[:, :, :], sl[:, :, :], eqr[:, :, :], ALU.add).then_inc(S["route_c"], 1)
            need(dve, "route_c", 1)
            need(dve, "route_e", 2)
            step(tt_(gt[:, :, :], sl[:, :, :], ex[:, :, :], ALU.mult))
            sync()
            step(V.tensor_reduce(out=nr[:, 2:4], in_=gt[:, :, :], op=ALU.add, axis=AX))
            sync()
            step(V.reciprocal(nr[:, 2:4], nr[:, 2:4]))
            sync()
            step(tt_(gt[:, :, :], gt[:, :, :], nr[:, 2:4].unsqueeze(2).broadcast_to([P, NT, NE]), ALU.mult))
            b = take(dve, "cn")
            pv = b[:, 0:2 * NE].rearrange("p (t e) -> p t e", t=2)
            step(tt_(pos[:, :, :], pv, sl[:, :, :], ALU.mult))
            step(V.tensor_scalar(nb[:, 0, :], b[:, 2 * NE:3 * NE], 0.5, None, ALU.is_gt))
            done(V.tensor_scalar(nb[:, 1, :], b[:, 2 * NE:3 * NE], P + 0.5, None, ALU.is_gt), "cn")
            need_sb(dve, "cn")
            sync()
            step(V.tensor_scalar(pos[:, :, :], pos[:, :, :], 1.0, None, ALU.subtract))
            step(tt_(nb[:, 0, :], nb[:, 0, :], nb[:, 1, :], ALU.add))
            sync()
            step(V.tensor_tensor_scan(cb[:, :], nb[:, 0, :], nb[:, 0, :], 0.0, ALU.add, ALU.max))
            sync()
            step(V.tensor_scalar(cmp[:, :], cb[:, :], pidx[:, 0:1], None, ALU.is_le))
            V.tensor_copy(tab[0:1, NITEM:NITEM + 1], cb[0:1, NE - 1:NE]).then_inc(S["tab_ready"], 1)
            sync()
            step(V.tensor_reduce(out=ecol[:, 0:1], in_=cmp[:, :], op=ALU.add, axis=AX))
            step(tt_(nb[:, 1, :], cmp[:, :], nb[:, 0, :], ALU.mult))
            sync()
            step(V.tensor_reduce(out=ecol[:, 1:2], in_=nb[:, 1, :], op=ALU.add, axis=AX))
            sync()
            step(tt_(ecol[:, 1:2], pidx[:, 0:1], ecol[:, 1:2], ALU.subtract))
            sync()
            V.tensor_scalar(ecol[:, 1:2], ecol[:, 1:2], float(P), None, ALU.mult).then_inc(S["route_t"], 1)
            b = take(dve, "it")
            done(V.tensor_copy(ebc[:, :, :], b[:, 0:2 * NITEM].rearrange("p (a i) -> p a i", a=2)), "it")
            need_sb(dve, "it")
            V.tensor_copy(tab[0:1, 0:NITEM], ebc[0:1, 0, :]).then_inc(S["tab_ready"], 1)
            step(tt_(oh[:, :, :], ebc[:, 0, :].unsqueeze(2).broadcast_to([P, NITEM, NE]),
                     iota[:, 0:NE].unsqueeze(1).broadcast_to([P, NITEM, NE]), ALU.is_equal))
            sync()
            for src, dst in ((pos, posI), (gt, gateI)):
                for t in range(NT):
                    step(tt_(pr[:, :, :], oh[:, :, :], src[:, t, :].unsqueeze(1).broadcast_to([P, NITEM, NE]), ALU.mult))
                    sync()
                    step(V.tensor_reduce(out=dst[:, t, :], in_=pr[:, :, :], op=ALU.add, axis=AX))
                    sync()
            for t in range(NT):
                step(tt_(posI[:, t, :], posI[:, t, :], ebc[:, 1, :], ALU.subtract))
            sync()
            dve.wait_ge(S["tab_ready"], 2)
            items = dve.value_load(tab[0:1, NITEM:NITEM + 1], min_val=1, max_val=NITEM - 1)
            f0, _ = loop_fill["e"]

            def select(i):
                for t in range(NT):
                    V.tensor_scalar(Sl[:, t, :], iota[:, :], posI[:, t, bass.ds(i, 1)], None, ALU.is_equal)
                for t in range(NT):
                    ins = V.tensor_scalar(Sp[:, t, :], iota[:, :], posI[:, t, bass.ds(i, 1)],
                                          gateI[:, t, bass.ds(i, 1)], ALU.is_equal, ALU.mult)
                ins.then_inc(S["sel_item"], 1)

            select(0)
            with dve.Fori(0, items) as i:
                def full(bi, r):
                    dve.wait_ge(bank_full[bi], i * EPER[bi] + (f0[bi] + r + 1))
                    return banks[bi]

                for g in range(2):
                    b = full(5 - g, g)
                    V.tensor_copy(xg[:, 4 * g:4 * g + 4, :], v4(b)).then_inc(bank_done[5 - g], 1)
                select(i + 1)
                for j in range(NJ):
                    bu = 2 + j % 2
                    b = full(bu, j // 2)
                    dve.wait_ge(bank_done[j % 2], i * EPER[j % 2] + (f0[j % 2] + j // 2 + 1))
                    tt_(av[:, j % 2, :], gs[:, j % 2, :], b[:, :], ALU.mult).then_inc(bank_done[bu], 1)
                dve.wait_ge(S["down_done"], i * NJ + (DOWN0 + NJ))
                V.tensor_copy(Ys[:, 512:1024], banks[7][:, :]).then_inc(bank_done[7], 1)
                for g in range(4):
                    b = full(g, EPER[g] - 1)
                    o = x[:, 2 * g:2 * g + 2, :]
                    tt_(o, o, v2(b), ALU.add).then_inc(bank_done[g], 1)
            for g in range(4):
                dve.wait_ge(bank_done[g], items * EPER[g] + f0[g])
            V.memset(cst[:, 6:7], 0.0).then_inc(S["x_final"], 1)
            need(dve, "fin_ready", 1)
            step(V.reciprocal(rs[:, :], rs[:, :]))
            sync()
            for k in range(KD):
                V.scalar_tensor_tensor(out=h[:, k, :], in0=x[:, k, :], scalar=col(VA, 32 + k), in1=rs[:, :],
                                       op0=ALU.mult, op1=ALU.mult).then_inc(S["h_ready"], 1)
            for t in range(NT):
                need(dve, "yscat", 2 * t + 2)
                V.tensor_copy(xt[:, t, 512:1024], banks[2 * t + 1][:, :]).then_inc(S["out_tok"], 1)


_INS = ["x", "w_in", "b_gate", "g_mix", "fox_f_bias", "dsa_kv_norm", "dsa_w_uk", "dsa_w_uv", "rwkv_mu",
        "rwkv_w0", "rwkv_w_up", "rwkv_a0", "rwkv_a_up", "rwkv_g_up", "rwkv_k_k", "rwkv_k_a", "rwkv_r_k",
        "rwkv_ln_g", "rwkv_ln_b", "vres_down", "vres_mu", "vres_up", "vres_v0", "p_fox", "p_dsa",
        "p_rwkv", "w_out", "g_ffn", "ffn_w_gate", "ffn_w_up", "ffn_w_down", "router_w", "router_b",
        "moe_w_gate", "moe_w_up", "moe_w_down", "g_final"]


def kernel(**inputs):
    import numpy as _np
    import concourse.bacc as _bacc
    from concourse import mybir as _mybir
    from concourse.bass_utils import run_bass_kernel_spmd as _run

    nc = _bacc.Bacc("TRN2", target_bir_lowering=False, num_devices=1)
    arrays, aps = {}, {}
    for name in _INS:
        v = _np.ascontiguousarray(inputs[name])
        arrays[f"in_{name}"] = v
        aps[name] = nc.dram_tensor(f"in_{name}", v.shape, _mybir.dt.from_np(v.dtype), kind="ExternalInput").ap()
    o = nc.dram_tensor("out_0", (1, T, D), F32, kind="ExternalOutput").ap()
    trunk(nc, aps, o)
    r = _run(nc, [arrays], core_ids=[0])
    return r.results[0]["out_0"]
```
